# Optimizing a Trainium2 kernel written in Bass

```python
import math
import jax, jax.numpy as jnp
from jax import lax
import numpy as np

D_MODEL = 1024
BATCH = 1
SEQ = 1024
DEPTH = 1

MIX_WIDTH = D_MODEL
ATTN_WIDTH = MIX_WIDTH // 2
POOL_WIDTH = MIX_WIDTH - ATTN_WIDTH
HEAD_DIM = 64
N_HEADS = ATTN_WIDTH // HEAD_DIM
POOL_WINDOWS = (2, 4, 8, 16)
N_POOL_GROUPS = len(POOL_WINDOWS)
POOL_GROUP = POOL_WIDTH // N_POOL_GROUPS
D_FF = 4 * D_MODEL
PLE_DIM = 256
Q_BLOCK = 128
LN_EPS = 1e-5
RMS_EPS = 1e-6
DN_ALPHA = float((2 * DEPTH) ** 0.25)
DN_BETA = float((8 * DEPTH) ** -0.25)
PROJ_WIDTH = 3 * ATTN_WIDTH + POOL_WIDTH


def layer_norm(x, g, b):
    xf = x.astype(jnp.float32)
    mu = jnp.mean(xf, axis=-1, keepdims=True)
    var = jnp.mean(jnp.square(xf - mu), axis=-1, keepdims=True)
    y = (xf - mu) * lax.rsqrt(var + LN_EPS)
    return (y * g.astype(jnp.float32) + b.astype(jnp.float32)).astype(x.dtype)

def stick_breaking_attention(q, k, v):
    B, H, S, Dh = q.shape
    n_blk = S // Q_BLOCK
    scale = 1.0 / math.sqrt(Dh)
    q_blocks = q.reshape(B, H, n_blk, Q_BLOCK, Dh).transpose(2, 0, 1, 3, 4)
    starts = jnp.arange(n_blk, dtype=jnp.int32) * Q_BLOCK
    k_pos = jnp.arange(S, dtype=jnp.int32)
    kf = k.astype(jnp.float32)
    vf = v.astype(jnp.float32)

    def one_block(args):
        q_blk, start = args
        z = jnp.einsum("bhqd,bhkd->bhqk", q_blk.astype(jnp.float32), kf) * scale
        q_pos = start + jnp.arange(Q_BLOCK, dtype=jnp.int32)
        mask = k_pos[None, :] < q_pos[:, None]
        log_not = jnp.where(mask, jax.nn.log_sigmoid(-z), 0.0)
        suffix = lax.cumsum(log_not, axis=3, reverse=True) - log_not
        weights = jnp.where(mask, jnp.exp(jax.nn.log_sigmoid(z) + suffix), 0.0)
        return jnp.einsum("bhqk,bhkd->bhqd", weights, vf)

    out = lax.map(one_block, (q_blocks, starts))
    return out.transpose(1, 2, 0, 3, 4).reshape(B, H, S, Dh)

def multiscale_pool(u, w_pool, pool_scale):
    B, S, _ = u.shape
    uf = u.astype(jnp.float32)
    csum = jnp.cumsum(uf, axis=1)
    pos = jnp.arange(S, dtype=jnp.int32)
    diffs = []
    for g, w in enumerate(POOL_WINDOWS):
        sl = slice(g * POOL_GROUP, (g + 1) * POOL_GROUP)
        cg = csum[..., sl]
        lag = jnp.pad(cg, ((0, 0), (w, 0), (0, 0)))[:, :S]
        count = jnp.minimum(pos + 1, w).astype(jnp.float32)[None, :, None]
        diffs.append((cg - lag) / count - uf[..., sl])
    d = jnp.stack(diffs, axis=2)
    y = jnp.einsum("bsgc,gcd->bsgd", d, w_pool.astype(jnp.float32))
    return y.reshape(B, S, POOL_WIDTH) * pool_scale.astype(jnp.float32)

def first_inputs(seed: int = 0) -> dict:
    key = jax.random.key(seed)
    ks = jax.random.split(key, 24)
    nrm = lambda k, shape, s: jax.random.normal(k, shape, jnp.float32) * s
    L = DEPTH
    x = jax.random.normal(ks[0], (BATCH, SEQ, D_MODEL), jnp.float32)
    p = jax.random.normal(ks[1], (L, BATCH, SEQ, PLE_DIM), jnp.float32)
    emb_ln_g = 1.0 + nrm(ks[2], (D_MODEL,), 0.02)
    emb_ln_b = nrm(ks[3], (D_MODEL,), 0.02)
    col_scale = jnp.concatenate([
        jnp.ones((2 * ATTN_WIDTH,), jnp.float32),
        jnp.full((ATTN_WIDTH + POOL_WIDTH,), DN_BETA, jnp.float32)])
    w_in = nrm(ks[4], (L, D_MODEL, PROJ_WIDTH), D_MODEL ** -0.5) * col_scale
    attn_out_g = 1.0 + nrm(ks[5], (L, ATTN_WIDTH), 0.02)
    w_pool = nrm(ks[6], (L, N_POOL_GROUPS, POOL_GROUP, POOL_GROUP), POOL_GROUP ** -0.5 * DN_BETA)
    pool_scale = 1.0 + nrm(ks[7], (L, POOL_WIDTH), 0.02)
    w_out = nrm(ks[8], (L, MIX_WIDTH, D_MODEL), MIX_WIDTH ** -0.5 * DN_BETA)
    ln1_g = 1.0 + nrm(ks[9], (L, D_MODEL), 0.02)
    ln1_b = nrm(ks[10], (L, D_MODEL), 0.02)
    w_up = nrm(ks[11], (L, D_MODEL, D_FF), D_MODEL ** -0.5 * DN_BETA)
    w_down = nrm(ks[12], (L, D_FF, D_MODEL), D_FF ** -0.5 * DN_BETA)
    ln2_g = 1.0 + nrm(ks[13], (L, D_MODEL), 0.02)
    ln2_b = nrm(ks[14], (L, D_MODEL), 0.02)
    w_ple = nrm(ks[15], (L, PLE_DIM, D_MODEL), PLE_DIM ** -0.5 * DN_BETA)
    w_ple_gate = nrm(ks[16], (L, D_MODEL, D_MODEL), D_MODEL ** -0.5)
    ln3_g = 1.0 + nrm(ks[17], (L, D_MODEL), 0.02)
    ln3_b = nrm(ks[18], (L, D_MODEL), 0.02)
    return {"x": x, "p": p, "emb_ln_g": emb_ln_g, "emb_ln_b": emb_ln_b,
            "w_in": w_in, "attn_out_g": attn_out_g, "w_pool": w_pool, "pool_scale": pool_scale,
            "w_out": w_out, "ln1_g": ln1_g, "ln1_b": ln1_b, "w_up": w_up, "w_down": w_down,
            "ln2_g": ln2_g, "ln2_b": ln2_b, "w_ple": w_ple, "w_ple_gate": w_ple_gate,
            "ln3_g": ln3_g, "ln3_b": ln3_b}

def first_block(x, p, emb_ln_g, emb_ln_b, w_in, attn_out_g, w_pool, pool_scale, w_out,
              ln1_g, ln1_b, w_up, w_down, ln2_g, ln2_b, w_ple, w_ple_gate, ln3_g, ln3_b):
    B, S, D = x.shape
    dt = x.dtype
    x = layer_norm(x, emb_ln_g, emb_ln_b)
    for i in range(DEPTH):
        proj = x @ w_in[i]
        q, k, v, u = jnp.split(proj, [ATTN_WIDTH, 2 * ATTN_WIDTH, 3 * ATTN_WIDTH], axis=-1)
        to_heads = lambda t: t.reshape(B, S, N_HEADS, HEAD_DIM).transpose(0, 2, 1, 3)
        o = stick_breaking_attention(to_heads(q), to_heads(k), to_heads(v))
        o = o * lax.rsqrt(jnp.mean(o * o, axis=-1, keepdims=True) + RMS_EPS)
        o = o.transpose(0, 2, 1, 3).reshape(B, S, ATTN_WIDTH) * attn_out_g[i].astype(jnp.float32)
        pooled = multiscale_pool(u, w_pool[i], pool_scale[i])
        mixed = jnp.concatenate([o, pooled], axis=-1).astype(dt) @ w_out[i]
        x = layer_norm(DN_ALPHA * x + mixed, ln1_g[i], ln1_b[i])
        h = jnp.square(jax.nn.relu(x @ w_up[i])) @ w_down[i]
        x = layer_norm(DN_ALPHA * x + h, ln2_g[i], ln2_b[i])
        ple = (p[i] @ w_ple[i]) * jax.nn.sigmoid(x @ w_ple_gate[i])
        x = layer_norm(DN_ALPHA * x + ple, ln3_g[i], ln3_b[i])
    return x


_first_inputs = first_inputs


def first_inputs(seed=0):
    import zlib

    import numpy as np

    out = dict(_first_inputs(seed))
    spreads = {}
    factors = {'emb_ln_g': 2.774,
     'emb_ln_b': 2.792,
     'attn_out_g': 34.875,
     'pool_scale': 42.191,
     'ln1_g': 7.969,
     'ln1_b': 8.075,
     'ln2_g': 7.829,
     'ln2_b': 8.179,
     'ln3_g': 8.266,
     'ln3_b': 8.353}
    for name, (base, spread) in spreads.items():
        noise = np.random.default_rng([zlib.crc32(name.encode()), seed]).standard_normal(out[name].shape)
        drawn = base * np.exp(spread * noise) if base else spread * noise
        out[name] = __import__('jax').numpy.asarray(drawn.astype(out[name].dtype))
    for name, factor in factors.items():
        out[name] = (out[name] * factor).astype(out[name].dtype)
    return out


_narrow_inputs = first_inputs


def first_inputs(seed=0):

    out = dict(_narrow_inputs(seed))
    wider = {'attn_out_g': 4.06,
     'pool_scale': 4.07,
     'ln2_g': 3.09,
     'ln2_b': 3.1,
     'ln3_g': 3.24,
     'ln3_b': 3.23}
    for name, times in wider.items():
        mean = out[name].mean()
        out[name] = (mean + times * (out[name] - mean)).astype(out[name].dtype)
    return out


CHUNK = 64
MIX_WIDTH_2 = D_MODEL
CONV_CH = MIX_WIDTH_2 // 2
CONV_WIDTH = 31
CONV_GROUPS = 8
HGRN_WIDTH = MIX_WIDTH_2 - CONV_CH
HGRN_HEADS = 4
HGRN_DK = HGRN_WIDTH // HGRN_HEADS
HGRN_DV = HGRN_WIDTH // HGRN_HEADS
IN_COLS = 2 * CONV_CH + 4 * HGRN_WIDTH
D_FF_2 = 4 * D_MODEL
GN_EPS = 1e-5


def _rms(x, w):
    xf = x.astype(jnp.float32)
    y = xf * lax.rsqrt(jnp.mean(xf * xf, axis=-1, keepdims=True) + RMS_EPS)
    return (y * w.astype(jnp.float32)).astype(x.dtype)

def _conv_mixer(u_val, u_gate, w_dw, b_dw, gn_gain, gn_bias):
    B, S, _ = u_val.shape
    u = u_val * jax.nn.sigmoid(u_gate)
    y = lax.conv_general_dilated(
        u, w_dw[:, None, :].astype(u.dtype), window_strides=(1,),
        padding=[(CONV_WIDTH - 1, 0)],
        dimension_numbers=("NWC", "WIO", "NWC"),
        feature_group_count=CONV_CH) + b_dw
    yf = y.astype(jnp.float32).reshape(B, S, CONV_GROUPS, CONV_CH // CONV_GROUPS)
    mu = jnp.mean(yf, axis=-1, keepdims=True)
    var = jnp.mean(jnp.square(yf - mu), axis=-1, keepdims=True)
    yf = ((yf - mu) * lax.rsqrt(var + GN_EPS)).reshape(B, S, CONV_CH)
    yf = yf * gn_gain.astype(jnp.float32) + gn_bias.astype(jnp.float32)
    return jax.nn.silu(yf).astype(u_val.dtype)

def _hgrn2(q, fl, i, g, lb, g_out):
    B, S, _ = q.shape
    N = S // CHUNK
    f32 = jnp.float32
    qf = jax.nn.silu(q.astype(f32))
    f = lb + (1.0 - lb) * jax.nn.sigmoid(fl.astype(f32))
    logf = jnp.log(f)
    k = 1.0 - f
    v = i.astype(f32)

    def to_chunks(t, d):
        return t.reshape(B, N, CHUNK, HGRN_HEADS, d).transpose(1, 0, 3, 2, 4)

    qc, kc, lc = to_chunks(qf, HGRN_DK), to_chunks(k, HGRN_DK), to_chunks(logf, HGRN_DK)
    vc = to_chunks(v, HGRN_DV)
    causal = jnp.tril(jnp.ones((CHUNK, CHUNK), dtype=bool))

    def step(state, inp):
        qb, kb, vb, lb_ = inp
        cum = jnp.cumsum(lb_, axis=2)
        diff = cum[:, :, :, None, :] - cum[:, :, None, :, :]
        decay = jnp.exp(jnp.where(causal[None, None, :, :, None], diff, -jnp.inf))
        att = jnp.einsum("bhtk,bhsk,bhtsk->bhts", qb, kb, decay)
        o = jnp.einsum("bhts,bhsv->bhtv", att, vb) + \
            jnp.einsum("bhtk,bhkv->bhtv", qb * jnp.exp(cum), state)
        last = cum[:, :, -1:, :]
        state = jnp.exp(last[:, :, 0, :])[..., None] * state + \
            jnp.einsum("bhsk,bhsv->bhkv", kb * jnp.exp(last - cum), vb)
        return state, o

    s0 = jnp.zeros((B, HGRN_HEADS, HGRN_DK, HGRN_DV), f32)
    _, oc = lax.scan(step, s0, (qc, kc, vc, lc))
    o = oc.transpose(1, 0, 3, 2, 4).reshape(B, S, HGRN_HEADS, HGRN_DV)
    o = _rms(o, g_out.reshape(HGRN_HEADS, HGRN_DV))
    o = o * jax.nn.silu(g.astype(f32).reshape(B, S, HGRN_HEADS, HGRN_DV))
    return o.reshape(B, S, HGRN_WIDTH).astype(q.dtype)

def second_inputs(seed: int = 0) -> dict:
    key = jax.random.key(seed)
    ks = jax.random.split(key, 20)
    nrm = jax.random.normal
    L, D = DEPTH, D_MODEL
    return {
        "x": nrm(ks[0], (BATCH, SEQ, D), jnp.float32),
        "c": nrm(ks[1], (BATCH, D), jnp.float32),
        "w_ada": nrm(ks[2], (L, D, 6 * D), jnp.float32) * D ** -0.5,
        "b_ada": nrm(ks[3], (L, 6 * D), jnp.float32) * 0.02,
        "lb_logits": nrm(ks[4], (L + 1, HGRN_WIDTH), jnp.float32) * 0.1,
        "g_pre_mix": 1.0 + 0.02 * nrm(ks[5], (L, D), jnp.float32),
        "w_in": nrm(ks[6], (L, D, IN_COLS), jnp.float32) * D ** -0.5,
        "b_in": nrm(ks[7], (L, IN_COLS), jnp.float32) * 0.02,
        "w_dw": nrm(ks[8], (L, CONV_WIDTH, CONV_CH), jnp.float32) * CONV_WIDTH ** -0.5,
        "b_dw": nrm(ks[9], (L, CONV_CH), jnp.float32) * 0.02,
        "gn_gain": 1.0 + 0.02 * nrm(ks[10], (L, CONV_CH), jnp.float32),
        "gn_bias": nrm(ks[11], (L, CONV_CH), jnp.float32) * 0.02,
        "g_hgrn_out": 1.0 + 0.02 * nrm(ks[12], (L, HGRN_WIDTH), jnp.float32),
        "w_out": nrm(ks[13], (L, MIX_WIDTH_2, D), jnp.float32) * MIX_WIDTH_2 ** -0.5,
        "g_post_mix": 1.0 + 0.02 * nrm(ks[14], (L, D), jnp.float32),
        "g_pre_ffn": 1.0 + 0.02 * nrm(ks[15], (L, D), jnp.float32),
        "w_up": nrm(ks[16], (L, D, D_FF_2), jnp.float32) * D ** -0.5,
        "w_down": nrm(ks[17], (L, D_FF_2, D), jnp.float32) * D_FF_2 ** -0.5,
        "g_post_ffn": 1.0 + 0.02 * nrm(ks[18], (L, D), jnp.float32),
    }

def second_block(x, c, w_ada, b_ada, lb_logits, g_pre_mix, w_in, b_in, w_dw, b_dw, gn_gain,
              gn_bias, g_hgrn_out, w_out, g_post_mix, g_pre_ffn, w_up, w_down, g_post_ffn):
    lb_all = jnp.cumsum(jax.nn.softmax(lb_logits.astype(jnp.float32), axis=0), axis=0)
    c_act = jax.nn.silu(c)
    for l in range(DEPTH):
        mod = c_act @ w_ada[l] + b_ada[l]
        sh_m, sc_m, gt_m, sh_f, sc_f, gt_f = [m[:, None, :] for m in jnp.split(mod, 6, axis=-1)]

        h = _rms(x, g_pre_mix[l]) * (1.0 + sc_m) + sh_m
        p = h @ w_in[l] + b_in[l]
        o0 = 2 * CONV_CH
        cv = _conv_mixer(p[..., :CONV_CH], p[..., CONV_CH:o0],
                         w_dw[l], b_dw[l], gn_gain[l], gn_bias[l])
        W = HGRN_WIDTH
        hg = _hgrn2(p[..., o0:o0 + W], p[..., o0 + W:o0 + 2 * W],
                    p[..., o0 + 2 * W:o0 + 3 * W], p[..., o0 + 3 * W:o0 + 4 * W],
                    lb_all[l], g_hgrn_out[l])
        y = jnp.concatenate([cv, hg], axis=-1) @ w_out[l]
        x = x + gt_m * _rms(y, g_post_mix[l])

        h = _rms(x, g_pre_ffn[l]) * (1.0 + sc_f) + sh_f
        y = jnp.square(jax.nn.relu(h @ w_up[l])) @ w_down[l]
        x = x + gt_f * _rms(y, g_post_ffn[l])
    return x


_first_inputs_2 = second_inputs


def second_inputs(seed=0):
    import zlib

    import numpy as np

    out = dict(_first_inputs_2(seed))
    spreads = {}
    factors = {'lb_logits': 8.0,
     'g_pre_mix': 4.89,
     'b_in': 4.216,
     'b_dw': 53.928,
     'gn_gain': 200.0,
     'gn_bias': 200.0,
     'g_hgrn_out': 63.8,
     'g_post_mix': 43.292,
     'g_pre_ffn': 59.916,
     'g_post_ffn': 80.921}
    for name, (base, spread) in spreads.items():
        noise = np.random.default_rng([zlib.crc32(name.encode()), seed]).standard_normal(out[name].shape)
        drawn = base * np.exp(spread * noise) if base else spread * noise
        out[name] = __import__('jax').numpy.asarray(drawn.astype(out[name].dtype))
    for name, factor in factors.items():
        out[name] = (out[name] * factor).astype(out[name].dtype)
    return out


_narrow_inputs_2 = second_inputs


def second_inputs(seed=0):

    out = dict(_narrow_inputs_2(seed))
    wider = {'gn_gain': 5.5, 'gn_bias': 5.96, 'g_hgrn_out': 3.39, 'g_pre_ffn': 3.09, 'g_post_ffn': 3.58}
    for name, times in wider.items():
        mean = out[name].mean()
        out[name] = (mean + times * (out[name] - mean)).astype(out[name].dtype)
    return out


N_MEM = 256
EPS = 1e-6
MLSTM_HEADS = 4
MLSTM_HEAD_DIM = D_MODEL // 4
MLSTM_WIDTH = MLSTM_HEADS * MLSTM_HEAD_DIM
QKV_BLOCK = 4
CONV_WIDTH_3 = 4
ATTN_HEADS = 8
ATTN_HEAD_DIM = D_MODEL // 16
ATTN_WIDTH_3 = ATTN_HEADS * ATTN_HEAD_DIM
ROPE_DIM = ATTN_HEAD_DIM // 4
ROPE_THETA = 500000.0
DILATED_PATTERNS = ((128, 1), (512, 4), (2048, 16))
BAND_BLOCK = 128
XATTN_HEADS = 4
XATTN_HEAD_DIM = D_MODEL // 8
XATTN_WIDTH = XATTN_HEADS * XATTN_HEAD_DIM

MIX_WIDTH_3 = MLSTM_WIDTH + ATTN_WIDTH_3 + XATTN_WIDTH
IN_SIZES = [MLSTM_WIDTH] * 3 + [ATTN_WIDTH_3] * 4 + [XATTN_WIDTH] * 2
IN_WIDTH = sum(IN_SIZES)
IN_OFFSETS = [int(o) for o in np.cumsum(IN_SIZES)[:-1]]


def rmsnorm(x, g):
    xf = x.astype(jnp.float32)
    y = xf * lax.rsqrt(jnp.mean(xf * xf, axis=-1, keepdims=True) + EPS)
    return (y * g.astype(jnp.float32)).astype(x.dtype)

def head_layernorm(h, g):
    hf = h.astype(jnp.float32)
    mu = jnp.mean(hf, axis=-1, keepdims=True)
    var = jnp.mean(jnp.square(hf - mu), axis=-1, keepdims=True)
    y = (hf - mu) * lax.rsqrt(var + EPS)
    b, s = h.shape[0], h.shape[1]
    return y.reshape(b, s, -1) * g.astype(jnp.float32)

def partial_rope(x):
    s = x.shape[1]
    half = ROPE_DIM // 2
    pos = jnp.arange(s, dtype=jnp.float32)
    inv = ROPE_THETA ** (-jnp.arange(0, ROPE_DIM, 2, dtype=jnp.float32) / ROPE_DIM)
    ang = pos[:, None] * inv[None, :]
    cos = jnp.cos(ang)[None, :, None, :]
    sin = jnp.sin(ang)[None, :, None, :]
    xf = x.astype(jnp.float32)
    x1, x2, xp = xf[..., :half], xf[..., half:ROPE_DIM], xf[..., ROPE_DIM:]
    out = jnp.concatenate([x1 * cos - x2 * sin, x2 * cos + x1 * sin, xp], axis=-1)
    return out.astype(x.dtype)

def causal_depthwise_conv(x, w, bias):
    out = lax.conv_general_dilated(
        x, w[:, None, :].astype(x.dtype), window_strides=(1,),
        padding=[(CONV_WIDTH_3 - 1, 0)],
        dimension_numbers=('NWC', 'WIO', 'NWC'),
        feature_group_count=x.shape[-1])
    return out + bias.astype(x.dtype)

def banded_causal_attention(q, k, v, steps):
    L, hd = q.shape[-2], q.shape[-1]
    lead = q.shape[:-2]
    nb = -(-L // BAND_BLOCK)
    Lp = nb * BAND_BLOCK
    pad = [(0, 0)] * len(lead) + [(0, Lp - L), (0, 0)]
    qb, kb, vb = (jnp.pad(t.astype(jnp.float32), pad).reshape(*lead, nb, BAND_BLOCK, hd)
                  for t in (q, k, v))

    def with_prev(t):
        prev = jnp.pad(t, [(0, 0)] * len(lead) + [(1, 0), (0, 0), (0, 0)])[..., :-1, :, :]
        return jnp.concatenate([prev, t], axis=-2)

    kw, vw = with_prev(kb), with_prev(vb)
    s = jnp.einsum('...qd,...kd->...qk', qb, kw) * (hd ** -0.5)
    qi = jnp.arange(BAND_BLOCK)[:, None]
    ci = jnp.arange(2 * BAND_BLOCK)[None, :]
    dist = BAND_BLOCK + qi - ci
    key_pos = (jnp.arange(nb)[:, None, None] - 1) * BAND_BLOCK + ci[None]
    valid = (dist >= 0)[None] & (dist <= steps)[None] & (key_pos >= 0)
    s = jnp.where(valid, s, -jnp.inf)
    m = jnp.max(s, axis=-1, keepdims=True)
    p = jnp.exp(s - m)
    l = jnp.sum(p, axis=-1)
    o = jnp.einsum('...qk,...kd->...qd', p, vw) / l[..., None]
    lse = m[..., 0] + jnp.log(l)
    o = o.reshape(*lead, Lp, hd)[..., :L, :]
    lse = lse.reshape(*lead, Lp)[..., :L]
    return o, lse

def dilated_attention(q, k, v):
    b, h, s, hd = q.shape
    outs, lses = [], []
    for window, dil in DILATED_PATTERNS:
        def split(t):
            return t.reshape(b, h, s // dil, dil, hd).swapaxes(2, 3)
        o, lse = banded_causal_attention(split(q), split(k), split(v), window // dil)
        outs.append(o.swapaxes(2, 3).reshape(b, h, s, hd))
        lses.append(lse.swapaxes(2, 3).reshape(b, h, s))
    w = jax.nn.softmax(jnp.stack(lses), axis=0)
    return jnp.einsum('pbhs,pbhsd->bhsd', w, jnp.stack(outs))

def mlstm_chunkwise(q, k, v, i_pre, f_pre):
    b, s, h, dh = q.shape
    nc = s // CHUNK

    def vec_chunks(t):
        return t.astype(jnp.float32).reshape(b, nc, CHUNK, h, dh).transpose(1, 0, 3, 2, 4)

    def gate_chunks(t):
        return t.astype(jnp.float32).reshape(b, nc, CHUNK, h).transpose(1, 0, 3, 2)

    qc, kc, vc = vec_chunks(q), vec_chunks(k), vec_chunks(v)
    li = gate_chunks(i_pre)
    lf = jax.nn.log_sigmoid(gate_chunks(f_pre))
    causal = jnp.tril(jnp.ones((CHUNK, CHUNK), dtype=bool))

    def step(carry, xs):
        C, n, m_prev = carry
        qt, kt, vt, li_c, lf_c = xs
        bcum = jnp.cumsum(lf_c, axis=-1)
        dlog = bcum[..., :, None] - bcum[..., None, :] + li_c[..., None, :]
        dlog = jnp.where(causal, dlog, -jnp.inf)
        a = bcum + m_prev[..., None]
        m = jnp.maximum(a, jnp.max(dlog, axis=-1))
        wts = jnp.exp(dlog - m[..., None]) * jnp.einsum('bhtd,bhsd->bhts', qt, kt)
        inter = jnp.exp(a - m)
        num = inter[..., None] * jnp.einsum('bhtd,bhde->bhte', qt, C) + \
            jnp.einsum('bhts,bhse->bhte', wts, vt)
        den = inter * jnp.einsum('bhtd,bhd->bht', qt, n) + jnp.sum(wts, axis=-1)
        h_out = num / jnp.maximum(jnp.abs(den), jnp.exp(-m))[..., None]
        b_last = bcum[..., -1]
        g_log = b_last[..., None] - bcum + li_c
        m_new = jnp.maximum(b_last + m_prev, jnp.max(g_log, axis=-1))
        g = jnp.exp(g_log - m_new[..., None])
        decay = jnp.exp(b_last + m_prev - m_new)
        C = decay[..., None, None] * C + jnp.einsum('bhsd,bhse->bhde', g[..., None] * kt, vt)
        n = decay[..., None] * n + jnp.einsum('bhs,bhsd->bhd', g, kt)
        return (C, n, m_new), h_out

    init = (jnp.zeros((b, h, dh, dh), jnp.float32), jnp.zeros((b, h, dh), jnp.float32),
            jnp.zeros((b, h), jnp.float32))
    _, hs = lax.scan(step, init, (qc, kc, vc, li, lf))
    return hs.transpose(1, 0, 3, 2, 4).reshape(b, s, h, dh)

def block_diag_proj(t, w):
    b, s, width = t.shape
    tb = t.reshape(b, s, width // QKV_BLOCK, QKV_BLOCK)
    return jnp.einsum('bsnc,ncd->bsnd', tb, w.astype(t.dtype)).reshape(b, s, width)

def hybrid_layer(x, mem, g_norm, w_in, conv_w, conv_b, w_q_blk, w_k_blk, w_v_blk,
                 w_gate, b_gate, g_head, skip, g_mem, w_mem_kv, w_out):
    b, s, _ = x.shape
    hn = rmsnorm(x, g_norm)
    proj = hn @ w_in.astype(hn.dtype)
    xm, zm, om, qa, ka, va, za, qx, zx = jnp.split(proj, IN_OFFSETS, axis=-1)

    xc = jax.nn.silu(causal_depthwise_conv(xm, conv_w, conv_b))
    q_m = block_diag_proj(xc, w_q_blk)
    k_m = block_diag_proj(xc, w_k_blk)
    v_m = block_diag_proj(xm, w_v_blk)
    gates = jnp.concatenate([q_m, k_m, v_m], axis=-1) @ w_gate.astype(q_m.dtype) + \
        b_gate.astype(q_m.dtype)
    i_pre, f_pre = gates[..., :MLSTM_HEADS], gates[..., MLSTM_HEADS:]
    mh = lambda t: t.reshape(b, s, MLSTM_HEADS, MLSTM_HEAD_DIM)
    h_m = mlstm_chunkwise(mh(q_m), mh(k_m) * (MLSTM_HEAD_DIM ** -0.5), mh(v_m), i_pre, f_pre)
    h_m = jax.nn.sigmoid(mh(om).astype(jnp.float32)) * h_m
    y_m = (head_layernorm(h_m, g_head) + skip.astype(jnp.float32) * xc.astype(jnp.float32)) * \
        jax.nn.silu(zm.astype(jnp.float32))
    y_m = y_m.astype(x.dtype)

    ah = lambda t: t.reshape(b, s, ATTN_HEADS, ATTN_HEAD_DIM)
    qa_h = partial_rope(ah(qa)).transpose(0, 2, 1, 3)
    ka_h = partial_rope(ah(ka)).transpose(0, 2, 1, 3)
    va_h = ah(va).transpose(0, 2, 1, 3)
    o_a = dilated_attention(qa_h, ka_h, va_h)
    y_a = o_a.transpose(0, 2, 1, 3).reshape(b, s, ATTN_WIDTH_3).astype(x.dtype) * jax.nn.silu(za)

    mem_n = rmsnorm(mem, g_mem)
    kv = mem_n @ w_mem_kv.astype(mem_n.dtype)
    kx, vx = kv[..., :XATTN_WIDTH], kv[..., XATTN_WIDTH:]
    qx_h = qx.reshape(b, s, XATTN_HEADS, XATTN_HEAD_DIM).astype(jnp.float32)
    kx_h = kx.reshape(b, -1, XATTN_HEADS, XATTN_HEAD_DIM).astype(jnp.float32)
    vx_h = vx.reshape(b, -1, XATTN_HEADS, XATTN_HEAD_DIM).astype(jnp.float32)
    sc = jnp.einsum('bshd,bmhd->bhsm', qx_h, kx_h) * (XATTN_HEAD_DIM ** -0.5)
    p = jax.nn.softmax(sc, axis=-1)
    o_x = jnp.einsum('bhsm,bmhd->bshd', p, vx_h).reshape(b, s, XATTN_WIDTH)
    y_x = o_x.astype(x.dtype) * jax.nn.silu(zx)

    y = jnp.concatenate([y_m, y_a, y_x], axis=-1) @ w_out.astype(x.dtype)
    return x + y

def third_inputs(seed: int = 0) -> dict:
    key = jax.random.key(seed)
    ks = jax.random.split(key, 20)
    f32 = jnp.float32
    L, D = DEPTH, D_MODEL
    nblk = MLSTM_WIDTH // QKV_BLOCK
    x = jax.random.normal(ks[0], (BATCH, SEQ, D), f32)
    mem = jax.random.normal(ks[1], (BATCH, N_MEM, D), f32)
    g_norm = 1.0 + 0.01 * jax.random.normal(ks[2], (L, D), f32)
    w_in = jax.random.normal(ks[3], (L, D, IN_WIDTH), f32) * D ** -0.5
    conv_w = jax.random.normal(ks[4], (L, CONV_WIDTH_3, MLSTM_WIDTH), f32) * CONV_WIDTH_3 ** -0.5
    conv_b = 0.01 * jax.random.normal(ks[5], (L, MLSTM_WIDTH), f32)
    w_q_blk = jax.random.normal(ks[6], (L, nblk, QKV_BLOCK, QKV_BLOCK), f32) * QKV_BLOCK ** -0.5
    w_k_blk = jax.random.normal(ks[7], (L, nblk, QKV_BLOCK, QKV_BLOCK), f32) * QKV_BLOCK ** -0.5
    w_v_blk = jax.random.normal(ks[8], (L, nblk, QKV_BLOCK, QKV_BLOCK), f32) * QKV_BLOCK ** -0.5
    w_gate = jax.random.normal(ks[9], (L, 3 * MLSTM_WIDTH, 2 * MLSTM_HEADS), f32) * \
        (3 * MLSTM_WIDTH) ** -0.5
    b_gate = jnp.concatenate([
        0.1 * jax.random.normal(ks[10], (L, MLSTM_HEADS), f32),
        jax.random.uniform(ks[11], (L, MLSTM_HEADS), f32, 3.0, 6.0)], axis=-1)
    g_head = 1.0 + 0.01 * jax.random.normal(ks[12], (L, MLSTM_WIDTH), f32)
    skip = 1.0 + 0.01 * jax.random.normal(ks[13], (L, MLSTM_WIDTH), f32)
    g_mem = 1.0 + 0.01 * jax.random.normal(ks[14], (L, D), f32)
    w_mem_kv = jax.random.normal(ks[15], (L, D, 2 * XATTN_WIDTH), f32) * D ** -0.5
    w_out = jax.random.normal(ks[16], (L, MIX_WIDTH_3, D), f32) * MIX_WIDTH_3 ** -0.5
    g_final = 1.0 + 0.01 * jax.random.normal(ks[17], (D,), f32)
    return {"x": x, "mem": mem, "g_norm": g_norm, "w_in": w_in, "conv_w": conv_w,
            "conv_b": conv_b, "w_q_blk": w_q_blk, "w_k_blk": w_k_blk, "w_v_blk": w_v_blk,
            "w_gate": w_gate, "b_gate": b_gate, "g_head": g_head, "skip": skip,
            "g_mem": g_mem, "w_mem_kv": w_mem_kv, "w_out": w_out, "g_final": g_final}

def third_block(x, mem, g_norm, w_in, conv_w, conv_b, w_q_blk, w_k_blk, w_v_blk,
              w_gate, b_gate, g_head, skip, g_mem, w_mem_kv, w_out, g_final):
    for l in range(DEPTH):
        x = hybrid_layer(x, mem, g_norm[l], w_in[l], conv_w[l], conv_b[l], w_q_blk[l],
                         w_k_blk[l], w_v_blk[l], w_gate[l], b_gate[l], g_head[l], skip[l],
                         g_mem[l], w_mem_kv[l], w_out[l])
    return rmsnorm(x, g_final)


_first_inputs_3 = third_inputs


def third_inputs(seed=0):
    import zlib

    import numpy as np

    out = dict(_first_inputs_3(seed))
    spreads = {}
    factors = {'g_norm': 6.092, 'conv_b': 8.0, 'g_head': 8.0, 'skip': 8.0, 'g_mem': 8.0, 'g_final': 5.743}
    for name, (base, spread) in spreads.items():
        noise = np.random.default_rng([zlib.crc32(name.encode()), seed]).standard_normal(out[name].shape)
        drawn = base * np.exp(spread * noise) if base else spread * noise
        out[name] = __import__('jax').numpy.asarray(drawn.astype(out[name].dtype))
    for name, factor in factors.items():
        out[name] = (out[name] * factor).astype(out[name].dtype)
    return out


_narrow_inputs_3 = third_inputs


def third_inputs(seed=0):

    out = dict(_narrow_inputs_3(seed))
    wider = {'g_head': 12.0, 'skip': 6.66, 'g_mem': 5.99, 'g_final': 6.46}
    for name, times in wider.items():
        mean = out[name].mean()
        out[name] = (mean + times * (out[name] - mean)).astype(out[name].dtype)
    return out


def setup_inputs(seed=0):
    out = dict(first_inputs(seed))
    for name, value in second_inputs(seed + 1).items():
        if name != "x":
            out[name + "_2"] = value
    for name, value in third_inputs(seed + 2).items():
        if name != "x":
            out[name + "_3"] = value
    return out


def reference(
    x, p, emb_ln_g, emb_ln_b, w_in, attn_out_g, w_pool, pool_scale, w_out, ln1_g, ln1_b, w_up,
    w_down, ln2_g, ln2_b, w_ple, w_ple_gate, ln3_g, ln3_b, c_2, w_ada_2, b_ada_2, lb_logits_2,
    g_pre_mix_2, w_in_2, b_in_2, w_dw_2, b_dw_2, gn_gain_2, gn_bias_2, g_hgrn_out_2, w_out_2,
    g_post_mix_2, g_pre_ffn_2, w_up_2, w_down_2, g_post_ffn_2, mem_3, g_norm_3, w_in_3,
    conv_w_3, conv_b_3, w_q_blk_3, w_k_blk_3, w_v_blk_3, w_gate_3, b_gate_3, g_head_3, skip_3,
    g_mem_3, w_mem_kv_3, w_out_3, g_final_3,
):
    x = first_block(
        x, p, emb_ln_g, emb_ln_b, w_in, attn_out_g, w_pool, pool_scale, w_out, ln1_g, ln1_b,
        w_up, w_down, ln2_g, ln2_b, w_ple, w_ple_gate, ln3_g, ln3_b,
    )
    x = second_block(
        x, c_2, w_ada_2, b_ada_2, lb_logits_2, g_pre_mix_2, w_in_2, b_in_2, w_dw_2, b_dw_2,
        gn_gain_2, gn_bias_2, g_hgrn_out_2, w_out_2, g_post_mix_2, g_pre_ffn_2, w_up_2,
        w_down_2, g_post_ffn_2,
    )
    return third_block(
        x, mem_3, g_norm_3, w_in_3, conv_w_3, conv_b_3, w_q_blk_3, w_k_blk_3, w_v_blk_3,
        w_gate_3, b_gate_3, g_head_3, skip_3, g_mem_3, w_mem_kv_3, w_out_3, g_final_3,
    )


_drawn_inputs = setup_inputs


def setup_inputs(seed=0):
    import zlib

    import numpy as np

    out = dict(_drawn_inputs(seed))
    spreads = {}
    factors = {'g_norm_3': 2.792, 'conv_b_3': 10.27, 'g_head_3': 5.899, 'g_mem_3': 2.978}
    for name, (base, spread) in spreads.items():
        noise = np.random.default_rng([zlib.crc32(name.encode()), seed]).standard_normal(out[name].shape)
        drawn = base * np.exp(spread * noise) if base else spread * noise
        out[name] = __import__('jax').numpy.asarray(drawn.astype(out[name].dtype))
    for name, factor in factors.items():
        out[name] = (out[name] * factor).astype(out[name].dtype)
    return out
```

```python
import numpy as np

import concourse.bass as bass
import concourse.mybir as mybir

F32 = mybir.dt.float32
F32R = mybir.dt.float32r
ALU = mybir.AluOpType
ACT = mybir.ActivationFunctionType
AX = mybir.AxisListType

P = 128
S = 1024
D = 1024
NT = S // P
NK = D // P
HALF = 512
COLS = 512
NBANK = 4
D_FF = 4096

ALPHA = float(2.0 ** 0.25)
N_HEADS = 8
HEAD_DIM = 64
POOL_WINDOWS = (2, 4, 8, 16)
PLE = 256
LN_EPS = 1e-5
EXP_LN = "natural_log_exp_and_others"
RMS_EPS = 1e-6


class Names:
    pass


class Link:

    def __init__(self, sem):
        self.sem, self.n = sem, 0

    def __call__(self, eng, ins):
        self.n += 1
        ins.then_inc(self.sem, 1)
        eng.wait_ge(self.sem, self.n)


class Weights:

    def __init__(self, nc, sem):
        self.loaded = [sem("weights_loaded_0"), sem("weights_loaded_1")]
        self.mm_done = sem("mm_done")
        self.bank_free = sem("bank_free")
        self.issued = 0
        self.used = 0
        self.outs = 0
        self.ends = []

    def plan(self, outs_per_chunk):
        for k in outs_per_chunk:
            self.ends.append((self.ends[-1] if self.ends else 0) + k)

    def load(self, eng, wbuf, ap):
        n = self.issued
        if n >= 2:
            eng.wait_ge(self.mm_done, self.ends[n - 2])
        k = ap.shape[1]
        dst = wbuf[:, n % 2, 0:k, 0:ap.shape[2]] if len(ap.shape) == 3 else wbuf[:, n % 2].rearrange("p (k h) n -> p k h n", h=2)
        eng.dma_start(dst, ap).then_inc(self.loaded[n % 2], 16)
        self.issued += 1


def chunk(w, c, rows=0):
    return w[rows:rows + D, c * COLS:(c + 1) * COLS].rearrange("(k p) n -> p k n", p=P)


def pe_chunk(pe, m, lhs, rhs, n_out, wait_before=None):
    wt = m.wt
    n = wt.used
    slot = m.wbuf[:, n % 2]
    pe.wait_ge(wt.loaded[n % 2], 16 * (n // 2 + 1))
    for g in range(n_out):
        G = wt.outs
        pe.wait_ge(wt.bank_free, G + 1)
        if wait_before:
            wait_before(g)
        for k in range(NK):
            r = rhs(slot, g, k)
            mm = pe.matmul(m.bank[:, G % NBANK, 0:r.shape[-1]], lhs(slot, g, k), r,
                           start=(k == 0), stop=(k == NK - 1))
        mm.then_inc(wt.mm_done, 1)
        wt.outs += 1
    wt.used += 1


def pe_feature_chunk(pe, m, xT, width=S, **kw):
    h = min(HALF, width)
    nh = width // h
    pe_chunk(pe, m, lambda w, g, k: w[:, k, (g // nh) * P:(g // nh + 1) * P],
             lambda w, g, k: xT[:, k, (g % nh) * h:(g % nh + 1) * h], 4 * nh, **kw)


def pe_token_chunk(pe, m, xT, tiles=NT, **kw):
    pe_chunk(pe, m, lambda w, g, k: xT[:, k, g * P:(g + 1) * P], lambda w, g, k: w[:, k, :], tiles, **kw)


def high_part(m, dve, hi, x):
    return dve.tensor_copy(m.parts(hi), x)


def low_part(m, dve, hi, x):
    return dve.tensor_tensor(m.parts(x), x, m.parts(hi).bitcast(F32), ALU.subtract)


def split_products(m, pe, out, lhs, rhs, first, last):
    pe.matmul(out, m.parts(lhs[0]), m.parts(rhs[0]), start=first, stop=False)
    pe.matmul(out, m.parts(lhs[0]), m.parts(rhs[1]), start=False, stop=False)
    return pe.matmul(out, m.parts(lhs[1]), m.parts(rhs[0]), start=False, stop=last)


def split_operand(dve, m, x, hi):
    m.dve_link(dve, high_part(m, dve, hi, x))
    low_part(m, dve, hi, x).then_inc(m.split_done, 1)


def split_weights(dve, m, n, hi):
    dve.wait_ge(m.wt.loaded[n % 2], 16 * (n // 2 + 1))
    split_operand(dve, m, m.wbuf[:, n % 2], hi)


def split_first(dve, m, x, x_high, n, w_high):
    split_operand(dve, m, x[:, :, 0:HALF], x_high[:, :, 0:HALF])
    split_weights(dve, m, n, w_high)
    split_operand(dve, m, x[:, :, HALF:S], x_high[:, :, HALF:S])


def pe_split_chunk(pe, m, x, x_high, w_high, at, feature, first=False, wait_before=None):
    wt = m.wt
    slot = m.wbuf[:, wt.used % 2]
    for g in range(8):
        pe.wait_ge(m.split_done, at - 1 if first and g == 0 else at)
        G = wt.outs
        pe.wait_ge(wt.bank_free, G + 1)
        if wait_before:
            wait_before(g)
        for k in range(NK):
            if feature:
                w = [t[:, k, (g // 2) * P:(g // 2 + 1) * P] for t in (w_high, slot)]
                v = [t[:, k, (g % 2) * HALF:(g % 2 + 1) * HALF] for t in (x_high, x)]
                mm = split_products(m, pe, m.bank[:, G % NBANK, :], w, v, k == 0, k == NK - 1)
            else:
                low = x(k) if callable(x) else x[:, k, :]
                v = [x_high[:, k, g * P:(g + 1) * P], low[:, g * P:(g + 1) * P]]
                mm = split_products(m, pe, m.bank[:, G % NBANK, :], v, [t[:, k, :] for t in (w_high, slot)], k == 0, k == NK - 1)
        mm.then_inc(wt.mm_done, 1)
        wt.outs += 1
    wt.used += 1


def quarter(t, h):
    return t[:, 4 * h:4 * h + 4, :].rearrange("p a (b n) -> p (a b) n", n=COLS)


def ln_stats(dve, m, i, src, link):
    link(dve, dve.bn_stats(m.stats[:, i % 2, 0, :], src[:, 0:HALF]))
    link(dve, dve.bn_stats(m.stats[:, i % 2, 1, :], src[:, HALF:D]))
    return dve.bn_aggr(m.mv[:, i % 2, :], m.stats[:, i % 2])


class Norm:

    def __init__(self, m, name, eps, scale_residual=True):
        self.m, self.eps, self.scale_residual = m, eps, scale_residual
        self.var_ready, self.root_ready, self.rows_ready, self.turned, self.copied = (
            m.sem(f"{name}_{s}") for s in ("var_ready", "root_ready", "rows_ready", "turned", "copied"))

    def vector(self, dve, i):
        m, x = self.m, self.m.X[:, i, :]
        st, mv = m.stats[:, i % 2], m.mv[:, i % 2]
        dve.bn_stats(st[:, 0, :], x[:, 0:HALF]).then_inc(m.dve_link.sem, 1)
        m.dve_link.n += 1
        m.dve_link(dve, dve.bn_stats(st[:, 1, :], x[:, HALF:D]))
        dve.bn_aggr(mv[:, 0:2], st.rearrange("p a b -> p (a b)")).then_inc(self.var_ready, 1)
        dve.wait_ge(self.root_ready, i + 1)
        m.dve_link(dve, dve.reciprocal(mv[:, 3:4], mv[:, 2:3]))
        m.dve_link(dve, dve.tensor_scalar(x, x, mv[:, 0:1], mv[:, 3:4], ALU.subtract, ALU.mult))
        m.dve_link(dve, dve.tensor_tensor(x, x, m.gb[:, 0, :], ALU.mult))
        dve.tensor_tensor(x, x, m.gb[:, 1, :], ALU.add).then_inc(self.rows_ready, 1)

    def tensor(self, pe, i):
        m = self.m
        pe.wait_ge(self.rows_ready, i + 1)
        for g in range(2):
            if i >= 1:
                pe.wait_ge(self.copied, 2 * i + g - 1)
            for k in range(4):
                t = pe.transpose(m.bank[:, 6 + g, k * P:(k + 1) * P],
                                 m.X[:, i, (4 * g + k) * P:(4 * g + k + 1) * P], m.ident)
            t.then_inc(self.turned, 1)

    LAG = 2

    def tensor_before(self, g):
        if g >= self.LAG:
            self.tensor(self.m.pe, g - self.LAG)

    def tensor_rest(self, pe):
        for i in range(NT - self.LAG, NT):
            self.tensor(pe, i)

    def scalar_root(self, act, i):
        m = self.m
        mv = m.mv[:, i % 2]
        act.wait_ge(self.var_ready, i + 1)
        act.activation(mv[:, 2:3], mv[:, 1:2], ACT.Sqrt, bias=m.eps_col(self.eps)).then_inc(self.root_ready, 1)

    def scalar_copy(self, act, i):
        m = self.m
        for g in range(2):
            act.wait_ge(self.turned, 2 * i + g + 1)
            act.activation(m.xT[:, 4 * g:4 * g + 4, i * P:(i + 1) * P],
                           m.bank[:, 6 + g, :].rearrange("p (k n) -> p k n", n=P),
                           ACT.Copy).then_inc(self.copied, 1)
        if self.scale_residual:
            act.activation(m.X[:, i, :], m.X[:, i, :], ACT.Copy, scale=ALPHA)


def load_gb(sp, m, g, b):
    n = 0
    for at, v in ((0, g), (1, b)):
        if v is not None:
            sp.dma_start(m.gb[:, at, :], v.partition_broadcast(P)).then_inc(m.gb_in, 16)
            n += 1
    m.gb_count += 16 * n


def embed_norm(nc, m, a, following):
    rows_in, rows_turned, x_in = m.sem("rows_in"), m.sem("rows_turned"), m.sem("x_in")
    rows = m.R[2][:, 0, 0:3 * P].rearrange("p (a n) -> p a n", n=P)
    norm = Norm(m, "embed", LN_EPS)
    n_rows_in = 2 + sum(len(v) for v in m.vectors)
    with nc.Block() as block:
        @block.sync
        def _(sp):
            load_gb(sp, m, a.emb_ln_g, a.emb_ln_b)
            sp.dma_start(m.X[:, 0, :], a.x[0, 0:P, :]).then_inc(x_in, 16)
            sp.dma_start(m.cst[:], a.consts).then_inc(rows_in, 16)
            for i in range(1, NT):
                sp.dma_start(m.X[:, i, :], a.x[0, i * P:(i + 1) * P, :]).then_inc(x_in, 16)
            sp.dma_start(m.poolfix[:], a.pool_fix).then_inc(rows_in, 16)
            for t in range(3):
                for ap, at, n in m.vectors[t]:
                    sp.dma_start(rows[at:at + n, t, :], ap).then_inc(rows_in, 16)
            for ap in following:
                m.wt.load(sp, m.wbuf, ap)

        @block.vector
        def _(dve):
            for v, e in enumerate((LN_EPS, RMS_EPS, 1.0)):
                dve.memset(m.eps[:, v:v + 1], e).then_inc(m.dve_link.sem, 1)
                m.dve_link.n += 1
            dve.wait_ge(m.dve_link.sem, m.dve_link.n)
            dve.sem_inc(m.wt.bank_free, NBANK)
            dve.wait_ge(m.gb_in, m.gb_count)
            for i in range(NT):
                dve.wait_ge(x_in, 16 * NT)
                norm.vector(dve, i)
            dve.wait_ge(rows_turned, 1)
            for t in range(3):
                dve.tensor_copy(m.col[:, m.col_at[t]:m.col_at[t] + m.n_rows[t]], m.bank[:, t, 0:m.n_rows[t]])

        @block.tensor
        def _(pe):
            pe.wait_ge(rows_in, 16 * n_rows_in)
            for t in range(3):
                n = m.n_rows[t]
                mm = pe.transpose(m.bank[:, t, 0:n], rows[0:n, t, :], m.cst[0:n, 0, 0:n])
            mm.then_inc(rows_turned, 1)
            for i in range(NT):
                norm.tensor(pe, i)

        @block.scalar
        def _(act):
            norm.scalar_root(act, 0)
            for i in range(NT):
                if i + 1 < NT:
                    norm.scalar_root(act, i + 1)
                norm.scalar_copy(act, i)


def project_1(nc, m, a, following):
    q, k, v, u = m.q1, m.k1, m.v1, m.u1
    wt = m.wt
    wt.plan([8] * 4)
    base = wt.outs
    x_high, w_high = m.R[4], [quarter(m.R[3], 0), quarter(m.R[3], 1), quarter(m.R[3], 1), m.wbuf[:, wt.used % 2]]
    with nc.Block() as block:
        @block.sync
        def _(sp):
            for c in range(wt.issued - wt.used, 4):
                wt.load(sp, m.wbuf, chunk(a.w_in, m.order1[c]))
            sp.wait_ge(wt.mm_done, base + 32)
            for ap in following:
                wt.load(sp, m.wbuf, ap)

        @block.tensor
        def _(pe):
            for c in range(4):
                pe_split_chunk(pe, m, m.xT, x_high, w_high[c], m.splits + 3 + c, c != 2, c == 0)

        @block.vector
        def _(dve):
            n0 = wt.used - 4
            split_first(dve, m, m.xT, x_high, n0, w_high[0])
            split_weights(dve, m, n0 + 1, w_high[1])
            for c in range(2, 4):
                dve.wait_ge(wt.mm_done, base + 8 * c)
                split_weights(dve, m, n0 + c, w_high[c])
            m.splits += 6

        @block.scalar
        def _(act):
            for g in range(32):
                c, o = g // 8, g % 8
                act.wait_ge(wt.mm_done, base + g + 1)
                src = m.bank[:, (base + g) % NBANK, :]
                if c == 2:
                    dst = v[:, o, :]
                else:
                    dst = (q, k, None, u)[c][:, o // 2, (o % 2) * HALF:(o % 2 + 1) * HALF]
                act.activation(dst, src, ACT.Copy, scale=HEAD_DIM ** -0.5 if c == 0 else 1.0).then_inc(wt.bank_free, 1)


def attention_1(nc, m, a, ada, following):
    wt = m.wt
    wt.plan([1] * 12)
    ada_base = wt.outs
    row = [m.R[4][0:1, 7, 0:HALF], m.R[4][0:1, 7, HALF:S]]
    c_exp, c_ready, = m.sem("c_exp"), m.sem("c_ready")
    row_out, col_done, mod_ready = m.sem("mod_row_out"), m.sem("mod_col_done"), m.sem("mod_ready")
    q, k, v, u, mixT = m.q1, m.k1, m.v1, m.u1, m.mixT
    units = []
    for pair in range(N_HEADS // 2):
        for half in range(2):
            for odd in range(2):
                top = 4 * half + 3
                for kt in range(top, -1, -1):
                    units.append((pair, half, odd, kt, top))
    n_units = len(units)
    first = {}
    last_of = {}
    for n, un in enumerate(units):
        last_of[un[0:2]] = n
    groups = sorted(last_of, key=lambda g: last_of[g])
    T = m.R[1][:].rearrange("p a b -> p (a b)")

    def slot(i):
        return T[:, i * HALF:(i + 1) * HALF]
    ea, sp_, aw, run = ([slot(b + i) for i in range(n)] for b, n in ((0, 3), (3, 3), (6, 3), (9, 2)))
    sq, rs = [slot(11), slot(12)], [slot(13), slot(14)]
    wpool = slot(15).rearrange("p (g c) -> p g c", c=P)
    pool_a, pool_b = m.gb[:, 0, :], m.gb[:, 1, :]
    z_ready, e_ready, sp_ready, run_ready, logit_ready = (m.sem(x) for x in ("z_ready", "softplus_log_ready", "softplus_ready", "running_sum_ready", "logit_ready"))
    diag_ready, a_ready, av_done = m.sem("diagonal_capped"), m.sem("attention_ready"), m.sem("values_done")
    o_done, sq_ready, ss_ready, rs_ready, mixed = (m.sem(x) for x in ("o_done", "o_squares_ready", "o_sums_ready", "o_rms_ready", "o_mixed"))
    wpool_in, diff_ready, pooled, pooled_out = (m.sem(x) for x in ("w_pool_in", "pool_diff_ready", "pooled", "pooled_out"))

    def cols(un):
        _, half, _, kt, top = un
        return max(0, kt * P - half * HALF)

    def is_diag(un):
        return un[3] * P >= un[1] * HALF
    n_diag = [sum(is_diag(x) for x in units[:n + 1]) for n in range(n_units)]

    with nc.Block() as block:
        @block.sync
        def _(sp):
            sp.dma_start(wpool, a.w_pool[0].rearrange("g c d -> c g d")).then_inc(wpool_in, 16)
            for ap in ada:
                wt.load(sp, m.wbuf, ap)
            for ap in following:
                wt.load(sp, m.wbuf, ap)

        @block.tensor
        def _(pe):
            def z(n):
                pair, half, odd, kt, top = units[n]
                b, c0 = 64 * odd, cols(units[n])
                if n >= 3:
                    pe.wait_ge(a_ready, n - 2)
                pe.matmul(m.bank[:, n % 3, c0:HALF], k[b:b + 64, pair, kt * P:(kt + 1) * P],
                          q[b:b + 64, pair, half * HALF + c0:(half + 1) * HALF],
                          start=True, stop=True).then_inc(z_ready, 1)

            def logit(n):
                pair, half, odd, kt, top = units[n]
                c0 = cols(units[n])
                c1 = c0 + P if is_diag(units[n]) else c0
                pe.wait_ge(sp_ready, n + 1)
                mm = pe.matmul(m.bank[:, n % 3, c0:HALF], m.negtri, sp_[n % 3][:, c0:HALF],
                               start=False, stop=True, skip_group_check=True)
                if kt != top and c1 < HALF:
                    pe.wait_ge(run_ready, n)
                    mm = pe.matmul(m.bank[:, n % 3, c1:HALF], m.negones, run[n % 2][:, c1:HALF],
                                   start=False, stop=True, skip_group_check=True)
                mm.then_inc(logit_ready, 1)

            def values(n):
                pair, half, odd, kt, top = units[n]
                c0, gi = cols(units[n]), groups.index((pair, half))
                h = 2 * pair + odd
                if kt == top and odd == 0 and gi >= 2:
                    pe.wait_ge(mixed, gi - 1)
                pe.wait_ge(a_ready, n + 1)
                pe.matmul(m.bank[64 * odd:64 * odd + 64, 4 + gi % 2, c0:HALF],
                          v[:, kt, h * 64:(h + 1) * 64], aw[n % 3][:, c0:HALF],
                          start=(kt == top), stop=(kt == 0), skip_group_check=True).then_inc(av_done, 1)

            def sums(gi):
                pe.wait_ge(sq_ready, gi + 1)
                if gi >= 1:
                    pe.wait_ge(rs_ready, gi)
                pe.matmul(m.bank[:, 6, :], m.headmean, sq[gi % 2], start=True, stop=True).then_inc(ss_ready, 1)

            def modulation(n):
                c, k = n // 8, n % 8
                if k == 0:
                    pe.wait_ge(wt.loaded[wt.used % 2], 16 * (wt.used // 2 + 1))
                    pe.wait_ge(wt.bank_free, NBANK + ada_base + c)
                    if c == 0:
                        pe.wait_ge(c_ready, 1)
                mm = pe.matmul(m.bank[0:1, 7, :], m.c_act[:, k:k + 1], m.wbuf[:, wt.used % 2, k, :],
                               start=(k == 0), stop=(k == NK - 1))
                if k == NK - 1:
                    mm.then_inc(wt.mm_done, 1)
                    wt.used += 1
                    wt.outs += 1
                if k == 3 and c >= 1:
                    columns(c - 1)

            def columns(c):
                pe.wait_ge(wt.bank_free, NBANK + ada_base + c + 1)
                for j in range(4):
                    mm = pe.matmul(m.bank[:, 3, 4 * c + j:4 * c + j + 1], row[c % 2][:, j * P:(j + 1) * P],
                                   m.ident[0:1, 0:1], start=True, stop=True)
                mm.then_inc(col_done, 1)

            pending = []
            for n in range(n_units + 2):
                if n < n_units:
                    z(n)
                    modulation(n)
                if 1 <= n <= n_units:
                    logit(n - 1)
                if n >= 2:
                    values(n - 2)
                    if pending and pending[0][0] <= n:
                        sums(pending.pop(0)[1])
                    if last_of[units[n - 2][0:2]] == n - 2:
                        pending.append((n + 2, groups.index(units[n - 2][0:2])))
            for _, gi in pending:
                sums(gi)
            columns(11)
            pe.wait_ge(wpool_in, 16)
            for g in range(4):
                pe.wait_ge(diff_ready, g + 1)
                for half in range(2):
                    n = 2 * g + half
                    if n < 3:
                        pe.wait_ge(a_ready, n_units)
                    else:
                        pe.wait_ge(pooled_out, n - 2)
                    pe.matmul(m.bank[:, n % 3, :], wpool[:, g, :], u[:, g, half * HALF:(half + 1) * HALF],
                              start=True, stop=True).then_inc(pooled, 1)

        @block.scalar
        def _(act):
            act.preload_act_table_set(EXP_LN)
            act.activation(m.c_act, m.cols("c", 0, 8), ACT.Exp, scale=-1.0).then_inc(c_exp, 1)

            def softplus_log(n):
                c0 = cols(units[n])
                e = ea[n % 3][:, c0:HALF]
                act.wait_ge(z_ready, n + 1)
                if n >= 3:
                    act.wait_ge(sp_ready, n - 2)
                m.act_link(act, act.activation(e, m.bank[:, n % 3, c0:HALF], ACT.Abs))
                m.act_link(act, act.activation(e, e, ACT.Exp, scale=-1.0))
                act.activation(e, e, ACT.Ln, bias=m.eps_col(1.0)).then_inc(e_ready, 1)

            def weights(n):
                c0 = cols(units[n])
                if is_diag(units[n]):
                    act.wait_ge(diag_ready, n_diag[n])
                else:
                    act.wait_ge(logit_ready, n + 1)
                if n >= 3:
                    act.wait_ge(av_done, n - 2)
                act.activation(aw[n % 3][:, c0:HALF], m.bank[:, n % 3, c0:HALF], ACT.Exp).then_inc(a_ready, 1)

            def squares(gi):
                act.wait_ge(av_done, last_of[groups[gi]] + 1)
                if gi >= 2:
                    act.wait_ge(ss_ready, gi - 1)
                act.activation(sq[gi % 2], m.bank[:, 4 + gi % 2, :], ACT.Square).then_inc(sq_ready, 1)

            def rms(gi):
                act.wait_ge(ss_ready, gi + 1)
                if gi >= 2:
                    act.wait_ge(mixed, gi - 1)
                m.act_link(act, act.activation(rs[gi % 2], m.bank[:, 6, :], ACT.Ln, bias=m.eps_col(RMS_EPS)))
                act.activation(rs[gi % 2], rs[gi % 2], ACT.Exp, scale=-0.5).then_inc(rs_ready, 1)

            pend_sq, pend_rms = [], []
            for n in range(n_units + 1):
                if n < n_units:
                    softplus_log(n)
                if n >= 1:
                    weights(n - 1)
                    if pend_rms and pend_rms[0][0] <= n:
                        rms(pend_rms.pop(0)[1])
                    if pend_sq and pend_sq[0][0] <= n:
                        gi = pend_sq.pop(0)[1]
                        squares(gi)
                        pend_rms.append((n + 2, gi))
                    if last_of[units[n - 1][0:2]] == n - 1:
                        pend_sq.append((n + 2, groups.index(units[n - 1][0:2])))
            for _, gi in pend_sq:
                squares(gi)
                pend_rms.append((0, gi))
            for _, gi in pend_rms:
                rms(gi)
            for n in range(8):
                act.wait_ge(pooled, n + 1)
                act.activation(mixT[:, 4 + n // 2, (n % 2) * HALF:(n % 2 + 1) * HALF], m.bank[:, n % 3, :],
                               ACT.Copy, scale=m.c("pool_scale", n // 2)).then_inc(pooled_out, 1)

        @block.vector
        def _(dve):
            def softplus(n):
                c0 = cols(units[n])
                s = sp_[n % 3]
                dve.wait_ge(e_ready, n + 1)
                if n >= 3:
                    dve.wait_ge(logit_ready, n - 2)
                    dve.wait_ge(run_ready, n - 2)
                ins = dve.scalar_tensor_tensor(s[:, c0:HALF], m.bank[:, n % 3, c0:HALF], 0.0, ea[n % 3][:, c0:HALF],
                                               op0=ALU.max, op1=ALU.add)
                if is_diag(units[n]):
                    m.dve_link(dve, ins)
                    ins = dve.tensor_tensor(s[:, c0:c0 + P], s[:, c0:c0 + P], m.before, ALU.mult)
                ins.then_inc(sp_ready, 1)

            def cap(n):
                if is_diag(units[n]):
                    c0 = cols(units[n])
                    dve.wait_ge(logit_ready, n + 1)
                    dve.tensor_tensor(m.bank[:, n % 3, c0:c0 + P], m.bank[:, n % 3, c0:c0 + P], m.cap,
                                      ALU.min).then_inc(diag_ready, 1)

            def mix(gi):
                pair, half = groups[gi]
                dve.wait_ge(rs_ready, gi + 1)
                dve.scalar_tensor_tensor(mixT[:, pair, half * HALF:(half + 1) * HALF], m.bank[:, 4 + gi % 2, :],
                                         m.c("attn_out_g", pair), rs[gi % 2], op0=ALU.mult,
                                         op1=ALU.mult).then_inc(mixed, 1)
            def row_copy(c):
                dve.wait_ge(wt.mm_done, ada_base + c + 1)
                if c >= 2:
                    dve.wait_ge(col_done, c - 1)
                dve.tensor_copy(row[c % 2], m.bank[0:1, 7, :]).then_inc(wt.bank_free, 1)

            dve.wait_ge(c_exp, 1)
            m.dve_link(dve, dve.tensor_scalar(m.c_act, m.c_act, 1.0, None, ALU.add))
            m.dve_link(dve, dve.reciprocal(m.c_act, m.c_act))
            dve.tensor_tensor(m.c_act, m.c_act, m.cols("c", 0, 8), ALU.mult).then_inc(c_ready, 1)
            pend = []
            for n in range(n_units + 1):
                if n >= 8 and n % 8 == 0:
                    row_copy(n // 8 - 1)
                if n < n_units:
                    softplus(n)
                if n >= 1:
                    cap(n - 1)
                    if pend and pend[0][0] <= n:
                        mix(pend.pop(0)[1])
                    if last_of[units[n - 1][0:2]] == n - 1:
                        pend.append((n + 5, groups.index(units[n - 1][0:2])))
            for _, gi in pend:
                mix(gi)
            dve.wait_ge(col_done, 12)
            m.dve_link(dve, dve.tensor_tensor(m.mod, m.bank[:, 3, 0:48], m.cols("b_ada", 0, 48), ALU.add))
            for at, g in ((8, "g_pre_mix"), (32, "g_pre_ffn")):
                part = m.mod[:, at:at + 8]
                m.dve_link(dve, dve.scalar_tensor_tensor(part, part, 1.0, m.cols(g, 0, 8), op0=ALU.add, op1=ALU.mult))

        @block.gpsimd
        def _(pool):
            steps = pool_steps(m, a, pool, u, pool_a, pool_b, diff_ready)
            for n in range(n_units):
                pair, half, odd, kt, top = units[n]
                c0 = cols(units[n])
                c1 = c0 + P if is_diag(units[n]) else c0
                src, dst, s = run[n % 2], run[(n + 1) % 2], sp_[n % 3]
                pool.wait_ge(sp_ready, n + 1)
                if n >= 1:
                    pool.wait_ge(logit_ready, n)
                    pool.wait_ge(run_ready, n)
                if kt == top:
                    pool.tensor_copy(dst[:, c0:HALF], s[:, c0:HALF]).then_inc(run_ready, 1)
                else:
                    if c1 > c0:
                        pool.tensor_copy(dst[:, c0:c1], s[:, c0:c1]).then_inc(m.pool_link.sem, 1)
                        m.pool_link.n += 1
                    pool.tensor_tensor(dst[:, c1:HALF], src[:, c1:HALF], s[:, c1:HALF], ALU.add)\
                        .then_inc(m.pool_link.sem, 1)
                    m.pool_link.n += 1
                    pool.wait_ge(m.pool_link.sem, m.pool_link.n)
                    pool.sem_inc(run_ready, 1)
                if n % 4 == 3 and steps:
                    steps.pop(0)()
            while steps:
                steps.pop(0)()


def pool_steps(m, a, pool, u, buf_a, buf_b, diff_ready):
    out = []
    for g, w in enumerate(POOL_WINDOWS):
        def shift_add(src, dst, d):
            def step():
                m.pool_link.n += 2
                pool.tensor_copy(dst[:, 0:d], src[:, 0:d]).then_inc(m.pool_link.sem, 1)
                pool.tensor_tensor(dst[:, d:S], src[:, d:S], src[:, 0:S - d], ALU.add).then_inc(m.pool_link.sem, 1)
                pool.wait_ge(m.pool_link.sem, m.pool_link.n)
            return step

        src, bufs, d = u[:, g, :], [buf_a, buf_b], 1
        while d < w:
            out.append(shift_add(src, bufs[0], d))
            src, bufs, d = bufs[0], bufs[::-1], 2 * d

        def finish(s=src, g=g, w=w):
            m.pool_link(pool, pool.tensor_tensor(s[:, 0:w], s[:, 0:w], m.poolfix[:, g, 0:w], ALU.mult))
            m.pool_link(pool, pool.tensor_scalar(s, s, 1.0 / w, None, ALU.mult))
            pool.tensor_tensor(u[:, g, :], s, u[:, g, :], ALU.subtract).then_inc(diff_ready, 1)
            pool.wait_ge(diff_ready, g + 1)
        out.append(finish)
    return out


def add_product(dve, m, i, n, base):
    x = m.X[:, i, n * COLS:(n + 1) * COLS]
    G = base + i
    dve.wait_ge(m.wt.mm_done, G + 1)
    return dve.tensor_tensor(x, x, m.bank[:, G % NBANK, :], ALU.add)


def mix_out_1(nc, m, a, following):
    wt, norm = m.wt, Norm(m, "ln1", LN_EPS)
    wt.plan([8, 8])
    base = wt.outs
    x_high, w_high = m.R[2], [quarter(m.R[3], h) for h in range(2)]
    with nc.Block() as block:
        @block.sync
        def _(sp):
            load_gb(sp, m, a.ln1_g, a.ln1_b)
            for ap in following:
                wt.load(sp, m.wbuf, ap)

        @block.tensor
        def _(pe):
            pe_split_chunk(pe, m, m.mixT, x_high, w_high[0], m.splits + 3, False, True)
            pe_split_chunk(pe, m, m.mixT, x_high, w_high[1], m.splits + 4, False, wait_before=norm.tensor_before)
            norm.tensor_rest(pe)

        @block.vector
        def _(dve):
            split_first(dve, m, m.mixT, x_high, wt.used - 2, w_high[0])
            split_weights(dve, m, wt.used - 1, w_high[1])
            m.splits += 4
            for i in range(NT):
                add_product(dve, m, i, 0, base).then_inc(wt.bank_free, 1)
            dve.wait_ge(m.gb_in, m.gb_count)
            for i in range(NT):
                add_product(dve, m, i, 1, base + NT).then_inc(wt.bank_free, 1)
                dve.wait_ge(wt.bank_free, NBANK + base + NT + i + 1)
                norm.vector(dve, i)

        @block.scalar
        def _(act):
            norm.scalar_root(act, 0)
            for i in range(NT):
                if i + 1 < NT:
                    norm.scalar_root(act, i + 1)
                norm.scalar_copy(act, i)


def down_chunk(w, j):
    return w[j * COLS:(j + 1) * COLS, :].rearrange("(k p) (h n) -> p k h n", p=P, h=2)


def feed_forward(nc, m, w_up, w_down, following, acc, tail, name, x_high, spilled=None, x_spill=None, zero=False):
    wt = m.wt
    parts = D_FF // COLS
    UP, DOWN = 8, 16
    OUTS = UP + DOWN
    high_ready, x_split, w_split, squared, h_ready, x_back = (m.sem(f"{name}_{x}") for x in (
        "high_ready", "x_split", "w_split", "squared", "h_ready", "x_back"))
    n0, base = wt.used, wt.outs
    assert wt.issued == n0 + 2 and n0 % 2 == 0 and base % NBANK == 0
    loaded0 = 16 * (n0 // 2)
    wt.plan([UP, DOWN] * parts)
    up_k = w_up.rearrange("(k p) n -> p k n", p=P)
    down_k = w_down.rearrange("(j k p) (h n) -> j p k h n", p=P, k=COLS // P, h=2)
    w_low = [m.wbuf[:, c] for c in range(2)]
    w_high = [m.R[4][:, 4 * c:4 * c + 4, :].rearrange("p a (b n) -> p (a b) n", n=COLS) for c in range(2)]
    xh = x_high[:].rearrange("p (h a) (b n) -> p h (a b) n", h=2, b=2)
    h_high, h_low = m.R[2][:, 0:4, :], m.R[2][:, 4:8, :]
    relu_of = [m.gb[:, 0, b * HALF:(b + 1) * HALF] for b in range(2)]

    def h_place(t, g):
        return t[:, g % 4, (g // 4) * HALF:(g // 4 + 1) * HALF]

    with nc.Block() as block:
        @block.sync
        def _(sp):
            def load(slot, mm_needed, dst, ap):
                sp.wait_ge(wt.mm_done, mm_needed)
                sp.dma_start(dst, ap).then_inc(wt.loaded[slot], 16)
            down_dst = m.wbuf[:, 1].rearrange("p (k h) n -> p k h n", h=2)
            with sp.Fori(0, parts - 1) as j:
                load(0, base + OUTS * j + UP, m.wbuf[:, 0], up_k[:, :, bass.ds(j * COLS + COLS, COLS)])
                load(1, base + OUTS * j + OUTS, down_dst, down_k[j + 1])
            wt.issued += 2 * parts - 2
            if x_spill is not None:
                for i in range(NT):
                    if i % 4 == 0:
                        sp.wait_ge(wt.mm_done, base + OUTS * (parts - 1) + 4 * (i // 4 + 1))
                    sp.dma_start(m.X[:, i, :], x_spill[i]).then_inc(x_back, 16)
            else:
                sp.wait_ge(squared, 2 + UP * parts)
            tail.sync(sp)
            for ap in following:
                wt.load(sp, m.wbuf, ap)
            if x_spill is not None:
                for i in range(NT):
                    sp.wait_ge(tail.x_ready, i + 1)
                    sp.dma_start(x_spill[i], m.X[:, i, :]).then_inc(spilled, 16)

        @block.tensor
        def _(pe):
            def part(j, before=None):
                pe.wait_ge(w_split, 2 * j + 1)
                for g in range(UP):
                    half, tile = g // 4, g % 4
                    pe.wait_ge(x_split, half + 1)
                    pe.wait_ge(wt.bank_free, base + OUTS * j + g + 1)
                    for k in range(NK):
                        mm = split_products(m, pe, m.bank[:, g % NBANK, :],
                                            [w[0][:, k, tile * P:(tile + 1) * P] for w in (w_high, w_low)],
                                            [xh[:, half, k, :], m.xT[:, k, half * HALF:(half + 1) * HALF]],
                                            k == 0, k == NK - 1)
                    mm.then_inc(wt.mm_done, 1)
                pe.wait_ge(w_split, 2 * j + 2)
                for g in range(DOWN):
                    i, n = g // 2, g % 2
                    if before and n == 0:
                        before(i)
                    if g % 8 == 0:
                        pe.wait_ge(h_ready, UP * j + 4 * (g // 8) + 4)
                    pe.wait_ge(wt.bank_free, base + OUTS * j + UP + g + 1)
                    for k in range(COLS // P):
                        mm = split_products(m, pe, m.bank[:, g % NBANK, :],
                                            [h[:, k, i * P:(i + 1) * P] for h in (h_high, h_low)],
                                            [w[1][:, 2 * k + n, :] for w in (w_high, w_low)],
                                            k == 0, k == COLS // P - 1)
                    mm.then_inc(wt.mm_done, 1)
            with pe.Fori(0, parts - 1) as j:
                part(j)
            part(parts - 1, tail.tensor_before)
            wt.used += 2 * parts
            wt.outs += OUTS * parts
            tail.tensor(pe)

        @block.vector
        def _(dve):
            def split(x, hi, n, done):
                high_part(m, dve, hi, x).then_inc(high_ready, 1)
                dve.wait_ge(high_ready, n + 1)
                low_part(m, dve, hi, x).then_inc(done, 1)

            def split_x(half, n):
                split(m.xT[:, :, half * HALF:(half + 1) * HALF], xh[:, half], n, x_split)

            def split_w(c, j, n):
                dve.wait_ge(wt.loaded[c], loaded0 + 16 * (j + 1))
                split(w_low[c], w_high[c], n, w_split)

            def relu(j, g):
                dve.wait_ge(wt.mm_done, base + OUTS * j + g + 1)
                dve.wait_ge(squared, UP * j + g + 1)
                dve.tensor_scalar(relu_of[g % 2], m.bank[:, g % NBANK, :], 0.0, None, ALU.max).then_inc(wt.bank_free, 1)

            def split_h(j, g, n):
                dve.wait_ge(squared, 2 + UP * j + g + 1)
                split(h_place(h_low, g), h_place(h_high, g), n, h_ready)

            def down(j, g):
                i, n = g // 2, g % 2
                x = acc[:, i, n * COLS:(n + 1) * COLS]
                dve.wait_ge(wt.mm_done, base + OUTS * j + UP + g + 1)
                dve.tensor_tensor(x, x, m.bank[:, g % NBANK, :], ALU.add).then_inc(wt.bank_free, 1)

            def up_part(j):
                h0 = 3 + 10 * j
                for g in range(UP):
                    relu(j, g)
                    if g:
                        split_h(j, g - 1, h0 + g - 1 + (g > 2))
                    if g == 2:
                        split_w(1, j, h0 + 2)
                split_h(j, UP - 1, h0 + UP)
            if spilled is not None:
                dve.wait_ge(spilled, 2 * 16 * NT)
            split_x(0, 0)
            split_w(0, 0, 1)
            split_x(1, 2)
            if zero:
                m.dve_link(dve, dve.memset(acc[:], 0.0))
            with dve.Fori(0, parts - 1) as j:
                up_part(j)
                for g in range(DOWN):
                    down(j, g)
                    if g == 7:
                        split_w(0, j + 1, 3 + 10 * j + 9)
            j = parts - 1
            up_part(j)
            tail.vector_before(dve)
            if x_spill is not None:
                dve.wait_ge(x_back, 16 * NT)
            for i in range(NT):
                down(j, 2 * i)
                down(j, 2 * i + 1)
                dve.wait_ge(wt.bank_free, NBANK + base + OUTS * j + UP + 2 * i + 2)
                tail.vector(dve, i)

        @block.scalar
        def _(act):
            act.sem_inc(squared, 2)

            def square(j, g):
                act.wait_ge(wt.bank_free, NBANK + base + OUTS * j + g + 1)
                act.activation(h_place(h_low, g), relu_of[g % 2], ACT.Square).then_inc(squared, 1)
            with act.Fori(0, parts - 1) as j:
                for g in range(UP):
                    square(j, g)
            for g in range(UP):
                square(parts - 1, g)
            tail.scalar(act)


class NormTail:

    def __init__(self, m, norm, g, b):
        self.m, self.norm, self.g, self.b = m, norm, g, b

    def sync(self, sp):
        load_gb(sp, self.m, self.g, self.b)

    def vector_before(self, dve):
        dve.wait_ge(self.m.gb_in, self.m.gb_count)

    def vector(self, dve, i):
        self.norm.vector(dve, i)

    def tensor_before(self, g):
        self.norm.tensor_before(g)

    def tensor(self, pe):
        self.norm.tensor_rest(pe)

    def scalar(self, act):
        self.norm.scalar_root(act, 0)
        for i in range(NT):
            if i + 1 < NT:
                self.norm.scalar_root(act, i + 1)
            self.norm.scalar_copy(act, i)


def per_layer_embedding(nc, m, a, following):
    wt = m.wt
    tail = Tail(m, "ln3", "layer norm", m.mod[:, 8:16], m.mod[:, 0:8], at=0)
    x_high, w_high = m.R[3], [quarter(m.R[4], h) for h in range(2)]
    wt.plan([8, 8])
    base = wt.outs
    p_in, turned, copied, ple_done, ple_free, gate_ready, gated = (m.sem(f"ple_{x}") for x in (
        "p_in", "turned", "copied", "done", "bank_free", "gate_ready", "gated"))
    p_rows = m.R[2][:, 0:2, :].rearrange("p a (b n) -> p (a b) n", n=PLE)
    p_T = m.R[2][:, 2:4, :]
    w_ple = m.R[2][:, 4:6, :]
    gate = [m.R[2][:, 6, 0:HALF], m.R[2][:, 6, HALF:S]]
    with nc.Block() as block:
        @block.sync
        def _(sp):
            sp.dma_start(p_rows, a.p[0, 0].rearrange("(i p) n -> p i n", p=P)).then_inc(p_in, 16)
            sp.dma_start(w_ple, a.w_ple[0].rearrange("(k p) n -> p k n", p=P)).then_inc(p_in, 16)
            load_gb(sp, m, a.ln3_g, a.ln3_b)
            for ap in following:
                wt.load(sp, m.wbuf, ap)
            for i in range(NT):
                sp.wait_ge(tail.x_ready, i + 1)
                sp.dma_start(a.x_spill[i], m.X[:, i, :]).then_inc(m.spilled, 16)

        @block.tensor
        def _(pe):
            pe.wait_ge(p_in, 32)
            for k in range(2):
                for half in range(2):
                    n = 2 * k + half
                    if n >= 2:
                        pe.wait_ge(copied, n - 1)
                    for i in range(4):
                        t = pe.transpose(m.bank[:, 6 + n % 2, i * P:(i + 1) * P],
                                         p_rows[:, 4 * half + i, k * P:(k + 1) * P], m.ident)
                    t.then_inc(turned, 1)
            pe.wait_ge(copied, 4)

            def ple(n):
                def go(g):
                    q = n * NT + g
                    if q >= 2:
                        pe.wait_ge(ple_free, q - 1)
                    for k in range(2):
                        mm = pe.matmul(m.bank[:, 4 + q % 2, :], p_T[:, k, g * P:(g + 1) * P],
                                       w_ple[:, k, n * COLS:(n + 1) * COLS], start=(k == 0), stop=(k == 1))
                    mm.then_inc(ple_done, 1)
                return go
            pe_split_chunk(pe, m, m.xT, x_high, w_high[0], m.splits + 3, False, True, wait_before=ple(0))
            ple_1 = ple(1)

            def before(g):
                ple_1(g)
                tail.tensor_before(g)
            pe_split_chunk(pe, m, m.xT, x_high, w_high[1], m.splits + 4, False, wait_before=before)
            tail.tensor(pe)

        @block.vector
        def _(dve):
            split_first(dve, m, m.xT, x_high, wt.used - 2, w_high[0])
            split_weights(dve, m, wt.used - 1, w_high[1])
            m.splits += 4

            def take(n, i):
                q = n * NT + i
                x = m.X[:, i, n * COLS:(n + 1) * COLS]
                dve.wait_ge(gate_ready, q + 1)
                dve.wait_ge(ple_done, q + 1)
                dve.tensor_tensor(gate[q % 2], gate[q % 2], m.bank[:, 4 + q % 2, :], ALU.mult).then_inc(ple_free, 1)
                dve.wait_ge(ple_free, q + 1)
                m.dve_link(dve, dve.tensor_tensor(x, x, gate[q % 2], ALU.add))
                dve.sem_inc(gated, 1)
            for i in range(NT):
                take(0, i)
            dve.wait_ge(m.gb_in, m.gb_count)
            for i in range(NT):
                take(1, i)
                tail.vector(dve, i)

        @block.scalar
        def _(act):
            for n in range(4):
                act.wait_ge(turned, n + 1)
                act.activation(p_T[:, n // 2, (n % 2) * HALF:(n % 2 + 1) * HALF], m.bank[:, 6 + n % 2, :],
                               ACT.Copy).then_inc(copied, 1)

            def gate_out(q):
                act.wait_ge(wt.mm_done, base + q + 1)
                if q >= 2:
                    act.wait_ge(gated, q - 1)
                act.activation(gate[q % 2], m.bank[:, (base + q) % NBANK, :], ACT.Sigmoid).then_inc(gate_ready, 1)
                act.wait_ge(gate_ready, q + 1)
                act.sem_inc(wt.bank_free, 1)
            for q in range(NT + 1):
                gate_out(q)
            tail.scalar(act, lambda i: gate_out(NT + i + 1) if i + 1 < NT else None)


class Tail:

    LAG = 3

    def __init__(self, m, name, kind, gain, offset, gate=None, at=1):
        self.m, self.kind, self.gain, self.offset, self.gate = m, kind, gain, offset, gate
        self.stat_ready, self.root_ready, self.x_ready, self.x_root, self.rows_ready, self.turned, self.copied = (
            m.sem(f"{name}_{s}") for s in ("stat_ready", "root_ready", "x_ready", "x_root", "rows_ready", "turned", "copied"))
        self.xh, self.junk = [m.R[4][:, at + b, :] for b in range(2)], [m.R[4][:, at + 2 + b, :] for b in range(2)]

    def sync(self, sp):
        pass

    def vector_before(self, dve):
        pass

    def vector(self, dve, i):
        m, x = self.m, self.m.X[:, i, :]
        mv = m.mv[:, i % 2]
        if self.kind == "layer norm":
            st = m.stats[:, i % 2]
            dve.bn_stats(st[:, 0, :], x[:, 0:HALF]).then_inc(m.dve_link.sem, 1)
            m.dve_link.n += 1
            m.dve_link(dve, dve.bn_stats(st[:, 1, :], x[:, HALF:D]))
            dve.bn_aggr(mv[:, 0:2], st.rearrange("p a b -> p (a b)")).then_inc(self.stat_ready, 1)
            dve.wait_ge(self.root_ready, i + 1)
            m.dve_link(dve, dve.reciprocal(mv[:, 3:4], mv[:, 2:3]))
            m.dve_link(dve, dve.tensor_scalar(x, x, mv[:, 0:1], mv[:, 3:4], ALU.subtract, ALU.mult))
            m.dve_link(dve, dve.tensor_tensor(x, x, m.gb[:, 0, :], ALU.mult))
            dve.tensor_tensor(x, x, m.gb[:, 1, :], ALU.add).then_inc(self.x_ready, 1)
        elif self.kind == "gated rms":
            y = m.Y[:, i, :]
            dve.sem_inc(self.stat_ready, 1)
            dve.wait_ge(self.root_ready, i + 1)
            m.dve_link(dve, dve.reciprocal(mv[:, 3:4], mv[:, 2:3]))
            m.dve_link(dve, dve.scalar_tensor_tensor(y, y, mv[:, 3:4], self.gate, op0=ALU.mult, op1=ALU.mult))
            dve.tensor_tensor(x, x, y, ALU.add).then_inc(self.x_ready, 1)
        else:
            dve.sem_inc(self.x_ready, 1)
        if i >= 1:
            self.rows(dve, i - 1)
        if i == NT - 1:
            self.rows(dve, i)

    def rows(self, dve, i):
        m = self.m
        xr = m.xroot[:, i % 2]
        dve.wait_ge(self.x_root, i + 1)
        if i >= 2:
            dve.wait_ge(self.turned, 2 * i - 2)
        m.dve_link(dve, dve.reciprocal(xr[:, 2:3], xr[:, 1:2]))
        dve.tensor_scalar(self.xh[i % 2], m.X[:, i, :], xr[:, 2:3], None, ALU.mult).then_inc(self.rows_ready, 1)

    def turn(self, pe, i):
        m = self.m
        pe.wait_ge(self.rows_ready, i + 1)
        for g in range(2):
            if i >= 1:
                pe.wait_ge(self.copied, 2 * i + g - 1)
            for k in range(4):
                t = pe.transpose(m.bank[:, 6 + g, k * P:(k + 1) * P],
                                 self.xh[i % 2][:, (4 * g + k) * P:(4 * g + k + 1) * P], m.ident)
            t.then_inc(self.turned, 1)

    def tensor_before(self, g):
        if g >= self.LAG:
            self.turn(self.m.pe, g - self.LAG)

    def tensor(self, pe):
        for i in range(NT - self.LAG, NT):
            self.turn(pe, i)

    def mean_square(self, act, src, i, out, ready):
        m = self.m
        m.act_link(act, act.activation(self.junk[i % 2], src, ACT.Square, accum_out=out[:, 0:1]))
        act.activation(out[:, 1:2], out[:, 0:1], ACT.Sqrt, scale=1.0 / D, bias=m.eps_col(RMS_EPS)).then_inc(ready, 1)

    def scalar_first(self, act, i):
        m = self.m
        mv = m.mv[:, i % 2]
        if self.kind == "layer norm":
            act.wait_ge(self.stat_ready, i + 1)
            act.activation(mv[:, 2:3], mv[:, 1:2], ACT.Sqrt, bias=m.eps_col(LN_EPS)).then_inc(self.root_ready, 1)
        elif self.kind == "gated rms":
            act.wait_ge(self.stat_ready, i + 1)
            self.mean_square(act, m.Y[:, i, :], i, mv[:, 1:3], self.root_ready)

    def scalar_copy(self, act, i):
        m = self.m
        for k in range(NK):
            if k % 4 == 0:
                act.wait_ge(self.turned, 2 * i + k // 4 + 1)
            ins = act.activation(m.xT[:, k, i * P:(i + 1) * P], m.bank[:, 6 + k // 4, (k % 4) * P:(k % 4 + 1) * P],
                                 ACT.Identity, scale=self.gain[:, k:k + 1],
                                 bias=self.offset[:, k:k + 1] if self.offset is not None else 0.0)
            if k % 4 == 3:
                ins.then_inc(self.copied, 1)

    def scalar(self, act, between=None):
        for i in range(NT + 2):
            if i < NT:
                self.scalar_first(act, i)
                if between:
                    between(i)
            if i >= 2:
                self.scalar_copy(act, i - 2)
            if i < NT:
                act.wait_ge(self.x_ready, i + 1)
                self.mean_square(act, self.m.X[:, i, :], i, self.m.xroot[:, i % 2], self.x_root)


CONV_W = 31
HG_HEADS = 4
LEVELS = (64, 32, 16, 8, 4, 2, 1)


def project_2(nc, m, a, following):
    wt = m.wt
    wt.plan([8] * 6)
    base = wt.outs
    val, gate = m.R[2][:, 0:4, :], m.R[2][:, 4:8, :]
    q, fl, iv, g = m.R[3][:, 0:4, :], m.R[3][:, 4:8, :], m.i2, m.R[4][:, 4:8, :]
    irow = m.gb[:, 0, 0:HALF]
    irow_in, val_ready, gated, tap = m.sem("b_i_in"), m.sem("conv_input_parts"), m.sem("conv_input"), m.sem("conv_tap")
    x_high, w_high = m.X, [quarter(m.R[4], (c + 1) % 2) for c in range(5)] + [m.wbuf[:, (wt.used + 4) % 2]]
    n0, split0 = wt.used, m.splits
    with nc.Block() as block:
        @block.sync
        def _(sp):
            sp.dma_start(irow, a.b_in_2[4 * HALF:5 * HALF].partition_broadcast(P)).then_inc(irow_in, 16)
            for c in range(wt.issued - wt.used, 6):
                wt.load(sp, m.wbuf, chunk(a.w_in_2, c))
            sp.wait_ge(wt.mm_done, base + 48)
            for ap in following:
                wt.load(sp, m.wbuf, ap)

        @block.tensor
        def _(pe):
            for c in range(6):
                pe_split_chunk(pe, m, m.xT, x_high, w_high[c], split0 + 3 + c, c != 4, c == 0)

        @block.scalar
        def _(act):
            for n in range(48):
                c, o = n // 8, n % 8
                act.wait_ge(wt.mm_done, base + n + 1)
                src = m.bank[:, (base + n) % NBANK, :]
                if c == 4:
                    act.activation(iv[:, o, :], src, ACT.Copy).then_inc(wt.bank_free, 1)
                    continue
                dst = (val, gate, q, fl, None, g)[c][:, o // 2, (o % 2) * HALF:(o % 2 + 1) * HALF]
                func = (ACT.Identity, ACT.Sigmoid, ACT.Silu, ACT.Sigmoid, None, ACT.Silu)[c]
                act.activation(dst, src, func, bias=m.c("b_in_2", 4 * c + o // 2)).then_inc(wt.bank_free, 1)

        @block.gpsimd
        def _(pool):
            for k in range(4):
                pool.wait_ge(wt.bank_free, NBANK + base + 8 + 2 * k + 2)
                pool.tensor_tensor(val[:, k, :], val[:, k, :], gate[:, k, :], ALU.mult).then_inc(gated, 1)
            pool.wait_ge(irow_in, 16)
            for i in range(NT):
                pool.wait_ge(wt.bank_free, NBANK + base + 32 + i + 1)
                pool.tensor_tensor(iv[:, i, :], iv[:, i, :], irow, ALU.add)

        @block.vector
        def _(dve):
            dve.wait_ge(m.spilled, 16 * NT)
            split_first(dve, m, m.xT, x_high, n0, w_high[0])

            def split(c):
                if c >= 2:
                    dve.wait_ge(wt.mm_done, base + 8 * (c - 1 if c < 5 else c))
                split_weights(dve, m, n0 + c, w_high[c])
            split(1)
            split(2)
            m.splits += 8
            n = 0
            for k in range(4):
                dve.wait_ge(gated, k + 1)
                dve.tensor_scalar(gate[:, k, :], val[:, k, :], m.c("w_dw", (CONV_W - 1) * 4 + k), m.c("b_dw", k),
                                  ALU.mult, ALU.add).then_inc(tap, 1)
                n += 1
            for lag in range(1, CONV_W):
                if lag in (2, 12, 24):
                    split({2: 3, 12: 4, 24: 5}[lag])
                for k in range(4):
                    dve.wait_ge(tap, n - 3)
                    y = gate[:, k, lag:S]
                    dve.scalar_tensor_tensor(y, val[:, k, 0:S - lag], m.c("w_dw", (CONV_W - 1 - lag) * 4 + k), y,
                                             op0=ALU.mult, op1=ALU.add).then_inc(tap, 1)
                    n += 1


def group_norm_and_hgrn(nc, m, a):
    y, cv, hg = m.R[2][:, 4:8, :], m.R[2][:, 0:4, :], m.R[2][:, 4:8, :]
    q, sig, g = m.R[3][:, 0:4, :], m.R[3][:, 4:8, :], m.R[4][:, 4:8, :]
    W = m.R[1]
    kk, cum = W[:, 0, :], W[:, 1, :]
    E, QS, KS = [W[:, 2, :], W[:, 3, :]], [W[:, 4, :], W[:, 5, :]], [W[:, 6, :], W[:, 7, :]]
    masks = m.gb[:, 0, :].rearrange("p (l t) -> p l t", t=P)
    att = [m.gb[:, 1, 0:HALF], m.gb[:, 1, HALF:S]]
    gd = [W[:, b, :] for b in range(4)]
    gs = [W[:, 4 + b, :] for b in range(4)]
    s = Names()
    s.masks_in, s.gn_mean_done, s.gn_centred, s.gn_squares = (
        m.sem("hg_masks_in"), m.sem("hg_gn_mean_done"), m.sem("hg_gn_centred"), m.sem("hg_gn_squares"))
    s.gn_var_done, s.gn_root, s.gn_scaled, s.gn_out = (
        m.sem("hg_gn_var_done"), m.sem("hg_gn_root"), m.sem("hg_gn_scaled"), m.sem("hg_gn_out"))
    s.lb_max, s.lb_exp, s.lb_ready, s.k_ready = (
        m.sem("hg_lb_max"), m.sem("hg_lb_exp"), m.sem("hg_lb_ready"), m.sem("hg_k_ready"))
    s.logf_ready, s.cum_ready, s.e_raw, s.e_ready = (
        m.sem("hg_logf_ready"), m.sem("hg_cum_ready"), m.sem("hg_e_raw"), m.sem("hg_e_ready"))
    s.qs_ready, s.ks_ready, s.att_done, s.masked = (
        m.sem("hg_qs_ready"), m.sem("hg_ks_ready"), m.sem("hg_att_done"), m.sem("hg_masked"))
    s.av_done, s.ke_turned, s.ke_copied, s.upd_done = (
        m.sem("hg_av_done"), m.sem("hg_ke_turned"), m.sem("hg_ke_copied"), m.sem("hg_upd_done"))
    s.state_ready, s.o_done, s.osq_ready, s.oss_done = (
        m.sem("hg_state_ready"), m.sem("hg_o_done"), m.sem("hg_osq_ready"), m.sem("hg_oss_done"))
    s.ors_ready, s.og_ready = (
        m.sem("hg_ors_ready"), m.sem("hg_og_ready"))
    NL = len(LEVELS) + 1
    lbt = m.lbt
    with nc.Block() as block:
        @block.sync
        def _(sp):
            sp.dma_start(masks, a.level_masks).then_inc(s.masks_in, 16)
            for i in range(NT):
                sp.dma_start(m.X[:, i, :], a.x_spill[i]).then_inc(m.x_back, 16)

        @block.tensor
        def _(pe):
            for k in range(4):
                for half in range(2):
                    n = 2 * k + half
                    if n >= 4:
                        pe.wait_ge(s.gn_centred, n - 3)
                    pe.matmul(m.bank[:, n % 4, :], m.headmean, y[:, k, half * HALF:(half + 1) * HALF],
                              start=True, stop=True).then_inc(s.gn_mean_done, 1)
            for n in range(8):
                pe.wait_ge(s.gn_squares, n + 1)
                if n >= 4:
                    pe.wait_ge(s.gn_root, n - 3)
                pe.matmul(m.bank[:, 4 + n % 4, :], m.headmean, gs[n // 2][:, (n % 2) * HALF:(n % 2 + 1) * HALF],
                          start=True, stop=True).then_inc(s.gn_var_done, 1)

            for h in range(HG_HEADS):
                def scores(l):
                    a_ = q[:, h, :] if l == 0 else QS[l % 2]
                    b_ = kk if l == 0 else KS[l % 2]
                    L = h * NL + l
                    if l == 0:
                        pe.wait_ge(s.k_ready, h + 1)
                        if h == 0:
                            pe.wait_ge(s.gn_scaled, 8)
                    else:
                        pe.wait_ge(s.qs_ready, h * NL + l)
                        pe.wait_ge(s.ks_ready, h * NL + l)
                    for half in range(2):
                        if L >= 2:
                            pe.wait_ge(s.masked, 2 * (L - 2) + half + 1)
                        for c in range(4):
                            t0 = (4 * half + c) * P
                            mm = pe.matmul(m.bank[:, 2 * (L % 2) + half, c * P:(c + 1) * P], b_[:, t0:t0 + P],
                                           a_[:, t0:t0 + P], start=True, stop=True)
                        mm.then_inc(s.att_done, 1)

                def values(l):
                    L = h * NL + l
                    for half in range(2):
                        pe.wait_ge(s.masked, 2 * L + half + 1)
                        if l == 0 and h >= 1:
                            pe.wait_ge(s.og_ready, 2 * (h - 1) + half + 1)
                        for c in range(4):
                            mm = pe.matmul(m.bank[:, 4 + half, c * P:(c + 1) * P],
                                           m.i2[:, 4 * half + c, h * P:(h + 1) * P], att[half][:, c * P:(c + 1) * P],
                                           start=(l == 0 and c == 0), stop=False, skip_group_check=True)
                        mm.then_inc(s.av_done, 1)
                for l in range(NL + 1):
                    if l < NL:
                        scores(l)
                    if l >= 1:
                        values(l - 1)
                pe.wait_ge(s.ks_ready, h * NL + NL)
                for half in range(2):
                    if h >= 1:
                        pe.wait_ge(s.ors_ready, 2 * (h - 1) + half + 1)
                    for c in range(4):
                        t0 = (4 * half + c) * P
                        mm = pe.transpose(m.bank[:, 6 + half, c * P:(c + 1) * P], KS[NL % 2][:, t0:t0 + P], m.ident)
                    mm.then_inc(s.ke_turned, 1)
                for half in range(2):
                    pe.wait_ge(s.ke_copied, 2 * h + half + 1)
                    for c in range(4 if half == 0 else 3):
                        mm = pe.matmul(m.bank[:, 6 + half, c * P:(c + 1) * P],
                                       sig[:, h, (4 * half + c) * P:(4 * half + c + 1) * P],
                                       m.i2[:, 4 * half + c, h * P:(h + 1) * P], start=True, stop=True)
                    mm.then_inc(s.upd_done, 1)
                pe.wait_ge(s.qs_ready, h * NL + NL)
                for half in range(2):
                    for c in range(4):
                        ch = 4 * half + c
                        if ch == 0:
                            continue
                        pe.wait_ge(s.state_ready, 7 * h + ch)
                        mm = pe.matmul(m.bank[:, 4 + half, c * P:(c + 1) * P], hg[:, h, ch * P:(ch + 1) * P],
                                       QS[NL % 2][:, ch * P:(ch + 1) * P], start=False, stop=True, skip_group_check=True)
                    mm.then_inc(s.o_done, 1)
                for half in range(2):
                    pe.wait_ge(s.osq_ready, 2 * h + half + 1)
                    pe.matmul(m.bank[:, 6 + half, :], m.ones, sig[:, h, half * HALF:(half + 1) * HALF],
                              start=True, stop=True).then_inc(s.oss_done, 1)

        @block.scalar
        def _(act):
            act.preload_act_table_set(EXP_LN)
            for n in range(8):
                act.wait_ge(s.gn_centred, n + 1)
                act.activation(gs[n // 2][:, (n % 2) * HALF:(n % 2 + 1) * HALF],
                               gd[n // 2][:, (n % 2) * HALF:(n % 2 + 1) * HALF], ACT.Square).then_inc(s.gn_squares, 1)
            for n in range(8):
                act.wait_ge(s.gn_var_done, n + 1)
                r = gs[n // 2][:, (n % 2) * HALF:(n % 2 + 1) * HALF]
                m.act_link(act, act.activation(r, m.bank[:, 4 + n % 4, :], ACT.Ln, bias=m.eps_col(LN_EPS)))
                act.activation(r, r, ACT.Exp, scale=-0.5).then_inc(s.gn_root, 1)
            act.wait_ge(s.lb_max, 1)
            act.activation(lbt[:, 4:12], lbt[:, 4:12], ACT.Exp).then_inc(s.lb_exp, 1)
            for n in range(8):
                k, half = n // 2, n % 2
                act.wait_ge(s.gn_scaled, n + 1)
                act.activation(cv[:, k, half * HALF:(half + 1) * HALF], gd[k][:, half * HALF:(half + 1) * HALF], ACT.Silu,
                               scale=m.c("gn_gain", k), bias=m.c("gn_bias", k)).then_inc(s.gn_out, 1)
            act.preload_act_table_set(EXP_LN)
            for h in range(HG_HEADS):
                act.wait_ge(s.k_ready, h + 1)
                act.activation(sig[:, h, :], sig[:, h, :], ACT.Ln).then_inc(s.logf_ready, 1)
                for l in range(1, NL + 2):
                    e = E[l % 2]
                    if l == NL:
                        act.wait_ge(s.cum_ready, h + 1)
                        act.wait_ge(s.qs_ready, h * NL + NL - 2)
                        act.wait_ge(s.ks_ready, h * NL + NL - 2)
                        act.activation(e, cum, ACT.Exp).then_inc(s.e_ready, 1)
                    else:
                        raw = h * NL + (l if l < NL else NL)
                        act.wait_ge(s.e_raw, raw)
                        act.activation(e, e, ACT.Exp).then_inc(s.e_ready, 1)
                for half in range(2):
                    act.wait_ge(s.ke_turned, 2 * h + half + 1)
                    act.activation(sig[:, h, half * HALF:(half + 1) * HALF], m.bank[:, 6 + half, :],
                                   ACT.Copy).then_inc(s.ke_copied, 1)
                for half in range(2):
                    act.wait_ge(s.o_done, 2 * h + half + 1)
                    act.wait_ge(s.upd_done, 2 * h + 2)
                    act.activation(sig[:, h, half * HALF:(half + 1) * HALF], m.bank[:, 4 + half, :],
                                   ACT.Square).then_inc(s.osq_ready, 1)
                for half in range(2):
                    r = sig[:, h, half * HALF:(half + 1) * HALF]
                    act.wait_ge(s.oss_done, 2 * h + half + 1)
                    m.act_link(act, act.activation(r, m.bank[:, 6 + half, :], ACT.Ln, scale=1.0 / P, bias=m.eps_col(RMS_EPS)))
                    act.activation(r, r, ACT.Exp, scale=-0.5).then_inc(s.ors_ready, 1)

        @block.gpsimd
        def _(pool):
            for h in range(HG_HEADS):
                for l in range(1, NL + 1):
                    pool.wait_ge(s.e_ready, h * (NL + 1) + (l if l < NL else NL + 1))
                    if l >= 3:
                        pool.wait_ge(s.att_done, 2 * (h * NL + l - 2) + 2)
                    elif h >= 1:
                        pool.wait_ge(s.ke_turned, 2 * h)
                    pool.tensor_tensor(KS[l % 2], kk, E[(NL + 1) % 2] if l == NL else E[l % 2],
                                       ALU.mult).then_inc(s.ks_ready, 1)

        @block.vector
        def _(dve):
            l0, l1, sc = m.cols("lb_logits", 0, 4), m.cols("lb_logits", 4, 4), lbt[:, 0:4]
            for n in range(8):
                k, half = n // 2, n % 2
                dve.wait_ge(s.gn_mean_done, n + 1)
                dve.tensor_tensor(gd[k][:, half * HALF:(half + 1) * HALF], y[:, k, half * HALF:(half + 1) * HALF],
                                  m.bank[:, n % 4, :], ALU.subtract).then_inc(s.gn_centred, 1)
            m.dve_link(dve, dve.tensor_tensor(sc, l0, l1, ALU.max))
            dve.tensor_tensor(lbt[:, 4:8], l0, sc, ALU.subtract).then_inc(m.dve_link.sem, 1)
            m.dve_link.n += 1
            m.dve_link(dve, dve.tensor_tensor(lbt[:, 8:12], l1, sc, ALU.subtract))
            dve.sem_inc(s.lb_max, 1)
            for n in range(8):
                d = gd[n // 2][:, (n % 2) * HALF:(n % 2 + 1) * HALF]
                dve.wait_ge(s.gn_root, n + 1)
                dve.tensor_tensor(d, d, gs[n // 2][:, (n % 2) * HALF:(n % 2 + 1) * HALF], ALU.mult).then_inc(s.gn_scaled, 1)
            dve.wait_ge(s.lb_exp, 1)
            m.dve_link(dve, dve.tensor_tensor(sc, lbt[:, 4:8], lbt[:, 8:12], ALU.add))
            m.dve_link(dve, dve.reciprocal(sc, sc))
            m.dve_link(dve, dve.tensor_tensor(lbt[:, 4:8], lbt[:, 4:8], sc, ALU.mult))
            m.dve_link(dve, dve.tensor_scalar(lbt[:, 8:12], lbt[:, 4:8], -1.0, 1.0, ALU.mult, ALU.add))
            dve.wait_ge(s.gn_out, 8)
            dve.wait_ge(s.masks_in, 16)

            def raw(h, l):
                e = E[l % 2] if l < NL else E[(NL + 1) % 2]
                if l == NL:
                    dve.wait_ge(s.qs_ready, h * NL + NL - 1)
                    dve.wait_ge(s.ks_ready, h * NL + NL - 1)
                    c3 = cum.rearrange("p (b t) -> p b t", t=P)
                    dve.tensor_tensor(e.rearrange("p (b t) -> p b t", t=P), c3[:, :, P - 1:P].broadcast_to([P, NT, P]),
                                      c3, ALU.subtract).then_inc(s.e_raw, 1)
                    return
                mm_ = LEVELS[l - 1]
                nb = S // (2 * mm_)
                if l >= 3:
                    dve.wait_ge(s.ks_ready, h * NL + l - 2)
                    dve.wait_ge(s.qs_ready, h * NL + l - 2)
                elif h >= 1:
                    dve.wait_ge(s.ks_ready, h * NL)
                    dve.wait_ge(s.qs_ready, h * NL)
                    dve.wait_ge(s.state_ready, 7 * h)
                c4 = cum.rearrange("p (b i t) -> p b i t", i=2, t=mm_)
                e4 = e.rearrange("p (b i t) -> p b i t", i=2, t=mm_)
                ref = c4[:, :, 0, mm_ - 1:mm_].broadcast_to([P, nb, mm_])
                dve.tensor_tensor(e4[:, :, 1, :], c4[:, :, 1, :], ref, ALU.subtract).then_inc(m.dve_link.sem, 1)
                m.dve_link.n += 1
                m.dve_link(dve, dve.tensor_tensor(e4[:, :, 0, :], ref, c4[:, :, 0, :], ALU.subtract))
                dve.sem_inc(s.e_raw, 1)

            def queries(h, l):
                dve.wait_ge(s.e_ready, h * (NL + 1) + l)
                if l >= 3:
                    dve.wait_ge(s.att_done, 2 * (h * NL + l - 2) + 2)
                elif h >= 1:
                    dve.wait_ge(s.o_done, 2 * h)
                dve.tensor_tensor(QS[l % 2], q[:, h, :], E[l % 2], ALU.mult).then_inc(s.qs_ready, 1)

            def mask(h, l):
                L = h * NL + l
                for half in range(2):
                    dve.wait_ge(s.att_done, 2 * L + half + 1)
                    if L >= 1:
                        dve.wait_ge(s.av_done, 2 * (L - 1) + half + 1)
                    dve.tensor_tensor(att[half].rearrange("p (c t) -> p c t", t=P),
                                      m.bank[:, 2 * (L % 2) + half, :].rearrange("p (c t) -> p c t", t=P),
                                      masks[:, l:l + 1, :].broadcast_to([P, 4, P]), ALU.mult).then_inc(s.masked, 1)

            for h in range(HG_HEADS):
                f = sig[:, h, :]
                m.dve_link(dve, dve.tensor_scalar(f, f, lbt[:, 8 + h:9 + h], lbt[:, 4 + h:5 + h], ALU.mult, ALU.add))
                if h >= 1:
                    dve.wait_ge(s.ks_ready, h * NL)
                    dve.wait_ge(s.att_done, 2 * (h - 1) * NL + 2)
                dve.tensor_scalar(kk, f, -1.0, 1.0, ALU.mult, ALU.add).then_inc(s.k_ready, 1)
                dve.wait_ge(s.logf_ready, h + 1)
                if h >= 1:
                    dve.wait_ge(s.e_ready, h * (NL + 1))
                for c in range(NT):
                    dve.tensor_tensor_scan(cum[:, c * P:(c + 1) * P], m.ones, f[:, c * P:(c + 1) * P], 0.0,
                                           ALU.mult, ALU.add).then_inc(m.dve_link.sem, 1)
                    m.dve_link.n += 1
                dve.wait_ge(m.dve_link.sem, m.dve_link.n)
                dve.sem_inc(s.cum_ready, 1)
                raw(h, 1)
                mask(h, 0)
                for l in range(1, NL):
                    if l + 1 < NL:
                        raw(h, l + 1)
                    queries(h, l)
                    if l >= 2:
                        mask(h, l - 1)
                raw(h, NL)
                mask(h, NL - 1)
                queries(h, NL)
                for ch in range(1, NT):
                    half = (ch - 1) // 4
                    c = (ch - 1) % 4
                    new = hg[:, h, ch * P:(ch + 1) * P]
                    if c == 0:
                        dve.wait_ge(s.upd_done, 2 * h + half + 1)
                    if ch == 1:
                        dve.tensor_copy(new, m.bank[:, 6 + half, 0:P]).then_inc(s.state_ready, 1)
                    else:
                        dve.wait_ge(s.state_ready, 7 * h + ch - 1)
                        dve.scalar_tensor_tensor(new, hg[:, h, (ch - 1) * P:ch * P], E[NL % 2][:, ch * P - 1:ch * P],
                                                 m.bank[:, 6 + half, c * P:(c + 1) * P], op0=ALU.mult,
                                                 op1=ALU.add).then_inc(s.state_ready, 1)
                for half in range(2):
                    r = sig[:, h, half * HALF:(half + 1) * HALF]
                    o = hg[:, h, half * HALF:(half + 1) * HALF]
                    dve.wait_ge(s.ors_ready, 2 * h + half + 1)
                    dve.wait_ge(s.o_done, 2 * h + 2)
                    m.dve_link(dve, dve.scalar_tensor_tensor(o, m.bank[:, 4 + half, :], m.c("g_hgrn_out", h), r,
                                                             op0=ALU.mult, op1=ALU.mult))
                    dve.tensor_tensor(o, o, g[:, h, half * HALF:(half + 1) * HALF], ALU.mult).then_inc(s.og_ready, 1)


def mix_out_2(nc, m, a, following):
    wt = m.wt
    tail = Tail(m, "post_mix", "gated rms", m.mod[:, 32:40], m.mod[:, 24:32], gate=m.gb[:, 0, :], at=0)
    x_high, w_high = m.R[1], [quarter(m.R[4], h) for h in range(2)]
    wt.plan([8, 8])
    base = wt.outs
    diag_ready, row_done, row_out, zeroed = m.sem("gate_diag"), m.sem("gate_row_done"), m.sem("gate_row"), m.sem("y_zeroed")
    diag = [m.R[4][:, 5, b * P:(b + 1) * P] for b in range(8)]
    with nc.Block() as block:
        @block.sync
        def _(sp):
            for ap in following:
                wt.load(sp, m.wbuf, ap)
            for i in range(NT):
                sp.wait_ge(tail.x_ready, i + 1)
                sp.dma_start(a.x_spill[i], m.X[:, i, :]).then_inc(m.spilled, 16)

        @block.tensor
        def _(pe):
            for n in range(16):
                pe.wait_ge(diag_ready, n + 1)
                if n >= 8 and n % 4 == 0:
                    pe.wait_ge(row_out, n // 4 - 1)
                mm = pe.matmul(m.bank[:, 4 + (n // 4) % 2, (n % 4) * P:(n % 4 + 1) * P], m.ones, diag[n % 8],
                               start=True, stop=True)
                if n % 4 == 3:
                    mm.then_inc(row_done, 1)
            pe_split_chunk(pe, m, m.R[2], x_high, w_high[0], m.splits + 3, False, True)
            pe_split_chunk(pe, m, m.R[2], x_high, w_high[1], m.splits + 4, False, wait_before=tail.tensor_before)
            tail.tensor(pe)

        @block.vector
        def _(dve):
            for r, (at, g) in enumerate(((16, "g_post_mix"), (40, "g_post_ffn"))):
                col = m.mod[:, at:at + 8]
                m.dve_link(dve, dve.tensor_tensor(col, col, m.cols(g, 0, 8), ALU.mult))
                for k in range(8):
                    n = 8 * r + k
                    if n >= 8 and n % 4 == 0:
                        dve.wait_ge(row_done, n // 4 - 1)
                    dve.tensor_scalar(diag[n % 8], m.ident, col[:, k:k + 1], None, ALU.mult).then_inc(diag_ready, 1)
            for n in range(4):
                dve.wait_ge(row_done, n + 1)
                dve.tensor_copy(m.gb[:, n // 2, (n % 2) * HALF:(n % 2 + 1) * HALF], m.bank[:, 4 + n % 2, :])\
                    .then_inc(row_out, 1)
            dve.wait_ge(row_out, 4)
            split_first(dve, m, m.R[2], x_high, wt.used - 2, w_high[0])
            split_weights(dve, m, wt.used - 1, w_high[1])
            m.splits += 4
            dve.wait_ge(m.x_back, 16 * NT)
            for n in range(2):
                for i in range(NT):
                    G = base + 8 * n + i
                    dve.wait_ge(wt.mm_done, G + 1)
                    dve.tensor_copy(m.Y[:, i, n * COLS:(n + 1) * COLS], m.bank[:, G % NBANK, :]).then_inc(wt.bank_free, 1)
                    if n == 1:
                        dve.wait_ge(wt.bank_free, NBANK + G + 1)
                        tail.vector(dve, i)

        @block.scalar
        def _(act):
            tail.scalar(act)


N_MEM = 256
MEM_T = N_MEM // P
A_HEADS, A_DIM = 8, 64
X_HEADS = 4
M_HEADS = 4
ROPE_DIM = 16
CHUNKS_3 = {"xm": (0, 1), "zm": (2, 3), "om": (4, 5), "qa": 6, "ka": 7, "va": 8, "za": 9, "qx": 10, "zx": 11}


def project_attention(nc, m, a, following):
    wt = m.wt
    wt.plan([8] * 4)
    base = wt.outs
    q, k, va, za = m.R[2][:, 0:4, :], m.R[2][:, 4:8, :], m.va, m.R[3][:, 4:8, :]
    cos, sin = m.R[4][:, 6, :], m.R[4][:, 7, :]
    swap = m.cst[:, 2, :]
    tmp = [m.gb[:, 0, 0:HALF], m.gb[:, 0, HALF:S]]
    tables_in, swapped, turned = m.sem("rope_tables_in"), m.sem("rope_swapped"), m.sem("rope_turned")
    x_high, w_high = m.X, [quarter(m.R[4], 0), quarter(m.R[3], 0), quarter(m.R[4], 0), m.wbuf[:, wt.used % 2]]
    n0, split0 = wt.used, m.splits
    with nc.Block() as block:
        @block.sync
        def _(sp):
            sp.dma_start(cos, a.rope[0]).then_inc(tables_in, 16)
            sp.dma_start(sin, a.rope[1]).then_inc(tables_in, 16)
            sp.dma_start(swap, a.rope_swap).then_inc(tables_in, 16)
            for n in range(wt.issued - wt.used, 4):
                wt.load(sp, m.wbuf, chunk(a.w_in_3, 6 + n))
            sp.wait_ge(wt.mm_done, base + 32)
            for ap in following:
                wt.load(sp, m.wbuf, ap)

        def part(u):
            t = (q, k)[u // 8][:, u % 8 // 2, :]
            return t[:, (u % 2) * HALF:(u % 2 + 1) * HALF]

        @block.tensor
        def _(pe):
            def rope(first):
                def go(g):
                    u = first + g
                    if u == 0:
                        pe.wait_ge(tables_in, 48)
                    pe.wait_ge(wt.bank_free, NBANK + base + u + 1)
                    if u >= 2:
                        pe.wait_ge(turned, u - 1)
                    pe.matmul(m.bank[:, 4 + u % 2, :], swap, part(u), start=True, stop=True).then_inc(swapped, 1)
                return go
            for c, before in enumerate((None, rope(0), rope(8), None)):
                pe_split_chunk(pe, m, m.xT, x_high, w_high[c], split0 + 3 + c, c != 2, c == 0, wait_before=before)

        @block.scalar
        def _(act):
            for n in range(32):
                c, o = n // 8, n % 8
                act.wait_ge(wt.mm_done, base + n + 1)
                src = m.bank[:, (base + n) % NBANK, :]
                if c < 2:
                    act.activation(part(n), src, ACT.Copy, scale=A_DIM ** -0.5 if c == 0 else 1.0).then_inc(wt.bank_free, 1)
                elif c == 2:
                    act.activation(va[:, o, :], src, ACT.Copy).then_inc(wt.bank_free, 1)
                else:
                    act.activation(za[:, o // 2, (o % 2) * HALF:(o % 2 + 1) * HALF], src, ACT.Silu).then_inc(wt.bank_free, 1)

        @block.vector
        def _(dve):
            dve.wait_ge(m.spilled, 3 * 16 * NT)
            split_first(dve, m, m.xT, x_high, n0, w_high[0])
            split_weights(dve, m, n0 + 1, w_high[1])
            dve.wait_ge(wt.mm_done, base + 8)
            split_weights(dve, m, n0 + 2, w_high[2])
            dve.wait_ge(tables_in, 48)
            for u in range(16):
                h = slice((u % 2) * HALF, (u % 2 + 1) * HALF)
                dve.wait_ge(swapped, u + 1)
                dve.tensor_tensor(tmp[u % 2], m.bank[:, 4 + u % 2, :], sin[:, h], ALU.mult).then_inc(m.dve_link.sem, 1)
                m.dve_link.n += 1
                m.dve_link(dve, dve.tensor_tensor(part(u), part(u), cos[:, h], ALU.mult))
                dve.tensor_tensor(part(u), part(u), tmp[u % 2], ALU.add).then_inc(turned, 1)
            dve.wait_ge(wt.mm_done, base + 24)
            split_weights(dve, m, n0 + 3, w_high[3])
            m.splits += 6


def dilated_attention(nc, m, a):
    q, k, va, y = m.R[2][:, 0:4, :], m.R[2][:, 4:8, :], m.va, m.R[3][:, 4:8, :]
    T = m.R[4]
    logc = T[:, 0, :]
    SB, PT = [T[:, 1, :], T[:, 2, :], T[:, 3, :]], [T[:, 4, :], T[:, 5, :]]
    units = [(h, t) for h in range(A_HEADS) for t in range(NT)]
    N = len(units)
    tab, s_done, max_ready, exp_ready, p_ready, turned, copied, o_done, y_ready = (m.sem(f"da_{x}") for x in (
        "table_in", "scores", "max", "exp", "weights", "turned", "copied", "out_done", "out"))
    restored = m.sem("x_whole")
    halves = lambda t: 1 if t < 4 else 2
    turns = [sum(halves(t) for _, t in units[:n + 1]) for n in range(N)]
    st = m.da_stat
    with nc.Block() as block:
        @block.sync
        def _(sp):
            sp.dma_start(logc, a.log_count).then_inc(tab, 16)
            sp.wait_ge(restored, 1)
            for i in range(NT):
                sp.dma_start(m.X[:, i, :], a.x_spill[i]).then_inc(m.x_back, 16)

        @block.gpsimd
        def _(pool):
            pool.tensor_tensor(m.xT[:], m.parts(m.xT[:]).bitcast(F32), m.parts(m.X[:]).bitcast(F32), ALU.add).then_inc(restored, 1)

        @block.tensor
        def _(pe):
            def scores(n):
                h, t = units[n]
                b, w = 64 * (h % 2), (t + 1) * P
                if n >= 2:
                    pe.wait_ge(max_ready, n - 1)
                for lo in range(0, w, HALF):
                    hi = min(w, lo + HALF)
                    mm = pe.matmul(m.bank[:, 2 * (n % 2) + lo // HALF, 0:hi - lo], q[b:b + 64, h // 2, t * P:(t + 1) * P],
                                   k[b:b + 64, h // 2, lo:hi], start=True, stop=True)
                mm.then_inc(s_done, 1)

            def turn(n):
                h, t = units[n]
                pe.wait_ge(p_ready, n + 1)
                for g in range(halves(t)):
                    prev = turns[n - 1] if n else 0
                    if n >= 1:
                        pe.wait_ge(copied, prev)
                    for j in range(4 * g, min(t + 1, 4 * g + 4)):
                        mm = pe.transpose(m.bank[:, 4 + g, (j % 4) * P:(j % 4 + 1) * P],
                                          SB[n % 3][:, j * P:(j + 1) * P], m.ident)
                    mm.then_inc(turned, 1)

            def out(n):
                h, t = units[n]
                b = 64 * (h % 2)
                pe.wait_ge(copied, turns[n])
                if n >= 2:
                    pe.wait_ge(y_ready, n - 1)
                for j in range(t + 1):
                    mm = pe.matmul(m.bank[b:b + 64, 6 + n % 2, 0:P], va[:, j, h * 64:(h + 1) * 64],
                                   PT[n % 2][:, j * P:(j + 1) * P], start=(j == 0), stop=(j == t))
                mm.then_inc(o_done, 1)
            for n in range(N + 3):
                if n < N:
                    scores(n)
                if 2 <= n < N + 2:
                    turn(n - 2)
                if n >= 3:
                    out(n - 3)

        @block.scalar
        def _(act):
            for n in range(N + 2):
                if n < N:
                    w = (units[n][1] + 1) * P
                    act.wait_ge(max_ready, n + 1)
                    act.activation(SB[n % 3][:, 0:w], SB[n % 3][:, 0:w], ACT.Exp, bias=st[:, n % 3, 1:2],
                                   accum_out=st[:, n % 3, 2:3]).then_inc(exp_ready, 1)
                if n >= 2:
                    u = n - 2
                    t = units[u][1]
                    if u >= 2:
                        act.wait_ge(o_done, u - 1)
                    for g in range(halves(t)):
                        w = min(t + 1 - 4 * g, 4) * P
                        act.wait_ge(turned, (turns[u - 1] if u else 0) + g + 1)
                        act.activation(PT[u % 2][:, g * HALF:g * HALF + w], m.bank[:, 4 + g, 0:w], ACT.Copy).then_inc(copied, 1)

        @block.vector
        def _(dve):
            def logits(n):
                h, t = units[n]
                w = (t + 1) * P
                x = st[:, n % 3]
                dve.wait_ge(s_done, n + 1)
                if n >= 3:
                    dve.wait_ge(turned, turns[n - 3])
                b = 2 * (n % 2)
                src = m.bank[:, b:b + 2, :].rearrange("p b n -> p (b n)")[:, 0:w]
                m.dve_link(dve, dve.tensor_tensor_reduce(SB[n % 3][:, 0:w], src, logc[:, (7 - t) * P:(7 - t) * P + w],
                                                         1.0, -3e38, ALU.add, ALU.max, x[:, 0:1]))
                dve.tensor_scalar(x[:, 1:2], x[:, 0:1], -1.0, None, ALU.mult).then_inc(max_ready, 1)

            def weights(n):
                w = (units[n][1] + 1) * P
                x = st[:, n % 3]
                dve.wait_ge(exp_ready, n + 1)
                m.dve_link(dve, dve.reciprocal(x[:, 3:4], x[:, 2:3]))
                dve.tensor_scalar(SB[n % 3][:, 0:w], SB[n % 3][:, 0:w], x[:, 3:4], None, ALU.mult).then_inc(p_ready, 1)

            def gate(n):
                h, t = units[n]
                b = 64 * (h % 2)
                o = y[b:b + 64, h // 2, t * P:(t + 1) * P]
                dve.wait_ge(o_done, n + 1)
                dve.tensor_tensor(o, m.bank[b:b + 64, 6 + n % 2, 0:P], o, ALU.mult).then_inc(y_ready, 1)
            dve.wait_ge(tab, 16)
            for n in range(N + 4):
                if n < N:
                    logits(n)
                if 1 <= n <= N:
                    weights(n - 1)
                if n >= 4:
                    gate(n - 4)


def cross_attention(nc, m, a, following):
    wt = m.wt
    wt.plan([4, MEM_T, 8, 8])
    base = wt.outs
    qx, y = m.R[2][:, 0:4, :], m.R[2][:, 4:8, :]
    T = m.R[4]
    mem = [T[:, i, :] for i in range(MEM_T)]
    memT = T[:, 2:4, :].rearrange("p a (k n) -> p (a k) n", n=N_MEM)
    kx = T[:, 4, :].rearrange("p (h n) -> p h n", n=N_MEM)
    vx = T[:, 5, :].rearrange("p (i n) -> p i n", n=HALF)
    SB, PT = [T[:, 6, :], T[:, 7, :]], [T[:, 0, :], T[:, 1, :]]
    st = m.da_stat.rearrange("p a b -> p (a b)")
    xs = m.xa_stat
    mem_in, sq, root, rows, turned, copied, s_done, max_ready, exp_ready, p_ready, w_turned, w_copied, o_done, y_ready = (
        m.sem(f"xa_{x}") for x in ("mem_in", "mean_square", "root", "rows", "turned", "copied", "scores", "max", "exp",
                                   "weights", "w_turned", "w_copied", "out_done", "out"))
    scale = 128 ** -0.5
    with nc.Block() as block:
        @block.sync
        def _(sp):
            for i in range(MEM_T):
                sp.dma_start(mem[i], a.mem_3[i * P:(i + 1) * P, :]).then_inc(mem_in, 16)
            for n in range(2, 4):
                wt.load(sp, m.wbuf, chunk(a.w_in_3, 8 + n))
            for ap in following:
                wt.load(sp, m.wbuf, ap)

        @block.tensor
        def _(pe):
            for i in range(MEM_T):
                pe.wait_ge(rows, i + 1)
                for g in range(2):
                    if i:
                        pe.wait_ge(copied, 2 * (i - 1) + g + 1)
                    for k in range(4):
                        t = pe.transpose(m.bank[:, 6 + g, k * P:(k + 1) * P], mem[i][:, (4 * g + k) * P:(4 * g + k + 1) * P],
                                         m.ident)
                    t.then_inc(turned, 1)
            pe.wait_ge(copied, 2 * MEM_T)
            pe_feature_chunk(pe, m, memT, width=N_MEM)
            pe_token_chunk(pe, m, memT, tiles=MEM_T)
            pe_feature_chunk(pe, m, m.xT)
            pe_feature_chunk(pe, m, m.xT)

            def scores(t):
                if t == 0:
                    pe.wait_ge(wt.bank_free, NBANK + base + 22)
                if t >= 2:
                    pe.wait_ge(exp_ready, t - 1)
                for h in range(X_HEADS):
                    mm = pe.matmul(m.bank[:, 2 * (t % 2) + h // 2, (h % 2) * N_MEM:(h % 2 + 1) * N_MEM],
                                   qx[:, h, t * P:(t + 1) * P], kx[:, h, :], start=True, stop=True)
                mm.then_inc(s_done, 1)

            def turn(t):
                pe.wait_ge(p_ready, t + 1)
                for g in range(2):
                    if t:
                        pe.wait_ge(w_copied, 2 * (t - 1) + g + 1)
                    for j in range(4):
                        mm = pe.transpose(m.bank[:, 4 + g, j * P:(j + 1) * P],
                                          SB[t % 2][:, (4 * g + j) * P:(4 * g + j + 1) * P], m.ident)
                    mm.then_inc(w_turned, 1)

            def out(t):
                pe.wait_ge(w_copied, 2 * t + 2)
                if t >= 2:
                    pe.wait_ge(y_ready, t - 1)
                for h in range(X_HEADS):
                    for j in range(MEM_T):
                        mm = pe.matmul(m.bank[:, 6 + t % 2, h * P:(h + 1) * P], vx[:, j, h * P:(h + 1) * P],
                                       PT[t % 2][:, (2 * h + j) * P:(2 * h + j + 1) * P], start=(j == 0), stop=(j == MEM_T - 1))
                mm.then_inc(o_done, 1)
            for n in range(NT + 2):
                if n < NT:
                    scores(n)
                if 1 <= n <= NT:
                    turn(n - 1)
                if n >= 2:
                    out(n - 2)

        @block.scalar
        def _(act):
            for i in range(MEM_T):
                act.wait_ge(mem_in, 16 * MEM_T)
                x = st[:, 3 * i:3 * i + 3]
                junk = m.R[4][:, 6 + i, :]
                m.act_link(act, act.activation(junk, mem[i], ACT.Square, accum_out=x[:, 0:1]))
                act.activation(x[:, 1:2], x[:, 0:1], ACT.Sqrt, scale=1.0 / D, bias=m.eps_col(RMS_EPS)).then_inc(root, 1)
            for i in range(MEM_T):
                for k in range(NK):
                    if k % 4 == 0:
                        act.wait_ge(turned, 2 * i + k // 4 + 1)
                    ins = act.activation(memT[:, k, i * P:(i + 1) * P], m.bank[:, 6 + k // 4, (k % 4) * P:(k % 4 + 1) * P],
                                         ACT.Copy, scale=m.c("g_mem", k))
                    if k % 4 == 3:
                        ins.then_inc(copied, 1)
            for n in range(22):
                G = base + n
                act.wait_ge(wt.mm_done, G + 1)
                src = m.bank[:, G % NBANK, :]
                if n < 4:
                    ins = act.activation(kx[:, n, :], src[:, 0:N_MEM], ACT.Copy)
                elif n < 6:
                    ins = act.activation(vx[:, n - 4, :], src, ACT.Copy)
                else:
                    o = (n - 6) % 8
                    dst = (qx, y)[(n - 6) // 8][:, o // 2, (o % 2) * HALF:(o % 2 + 1) * HALF]
                    ins = act.activation(dst, src, (ACT.Copy, ACT.Silu)[(n - 6) // 8])
                ins.then_inc(wt.bank_free, 1)
            for n in range(NT + 1):
                if n < NT:
                    act.wait_ge(max_ready, n + 1)
                    if n >= 2:
                        act.wait_ge(w_turned, 2 * (n - 2) + 2)
                    for h in range(X_HEADS):
                        ins = act.activation(SB[n % 2][:, h * N_MEM:(h + 1) * N_MEM],
                                             m.bank[:, 2 * (n % 2) + h // 2, (h % 2) * N_MEM:(h % 2 + 1) * N_MEM],
                                             ACT.Exp, scale=scale, bias=xs[:, n % 2, h:h + 1], accum_out=xs[:, n % 2, 4 + h:5 + h])
                    ins.then_inc(exp_ready, 1)
                if n >= 1:
                    u = n - 1
                    if u >= 2:
                        act.wait_ge(o_done, u - 1)
                    for g in range(2):
                        act.wait_ge(w_turned, 2 * u + g + 1)
                        act.activation(PT[u % 2][:, g * HALF:(g + 1) * HALF], m.bank[:, 4 + g, :], ACT.Copy).then_inc(w_copied, 1)

        @block.vector
        def _(dve):
            for i in range(MEM_T):
                x = st[:, 3 * i:3 * i + 3]
                dve.wait_ge(root, i + 1)
                m.dve_link(dve, dve.reciprocal(x[:, 2:3], x[:, 1:2]))
                dve.tensor_scalar(mem[i], mem[i], x[:, 2:3], None, ALU.mult).then_inc(rows, 1)
            for n in range(NT + 2):
                if n < NT:
                    x = xs[:, n % 2]
                    dve.wait_ge(s_done, n + 1)
                    if n >= 2:
                        dve.wait_ge(p_ready, n - 1)
                        dve.wait_ge(exp_ready, n - 1)
                    src = m.bank[:, 2 * (n % 2):2 * (n % 2) + 2, :].rearrange("p b (h n) -> p (b h) n", n=N_MEM)
                    m.dve_link(dve, dve.tensor_reduce(x[:, 0:4], src, AX.X, ALU.max))
                    dve.tensor_scalar(x[:, 0:4], x[:, 0:4], -scale, None, ALU.mult).then_inc(max_ready, 1)
                if 1 <= n <= NT:
                    u = n - 1
                    x = xs[:, u % 2]
                    dve.wait_ge(exp_ready, u + 1)
                    m.dve_link(dve, dve.reciprocal(x[:, 8:12], x[:, 4:8]))
                    sb = SB[u % 2].rearrange("p (h n) -> p h n", n=N_MEM)
                    dve.tensor_tensor(sb, sb, x[:, 8:12].unsqueeze(2).broadcast_to([P, X_HEADS, N_MEM]), ALU.mult).then_inc(p_ready, 1)
                if n >= 2:
                    u = n - 2
                    o = y[:, :, u * P:(u + 1) * P]
                    dve.wait_ge(o_done, u + 1)
                    dve.tensor_tensor(o, m.bank[:, 6 + u % 2, :].rearrange("p (h n) -> p h n", n=P), o, ALU.mult).then_inc(y_ready, 1)


def attention_out(nc, m, a, following):
    wt = m.wt
    wt.plan([8] * 4)
    base = wt.outs
    xm, xc, q = m.R[4], m.R[3], m.R[2]
    bd = [m.cst[:, t, :] for t in (2, 3, 4)]
    vT = [m.gb[:, b // 2, (b % 2) * HALF:(b % 2 + 1) * HALF] for b in range(4)]
    CW = 4
    s = Names()
    s.small_in, s.conv_ready, s.xc_ready, s.bd_ready = (
        m.sem("ml_small_in"), m.sem("ml_conv_ready"), m.sem("ml_xc_ready"), m.sem("ml_bd_ready"))
    s.blk_done, s.v_done, s.qk_ready, s.vt_ready = (
        m.sem("ml_blk_done"), m.sem("ml_v_done"), m.sem("ml_qk_ready"), m.sem("ml_vt_ready"))
    s.v_ready, s.gates_done, s.spilled = (
        m.sem("ml_v_ready"), m.sem("ml_gates_done"), m.sem("ml_spilled"))
    m.ml_gates_done = s.gates_done

    w_high = [quarter(m.R[2], 0), quarter(m.R[3], 0)]
    n0, split0 = wt.used, m.splits

    def half_of(t, k, half):
        return t[:, k, half * HALF:(half + 1) * HALF]

    with nc.Block() as block:
        @block.sync
        def _(sp):
            sp.dma_start(m.mask4, a.mask4).then_inc(s.small_in, 16)
            for n, w in enumerate((a.w_q_blk_3, a.w_k_blk_3, a.w_v_blk_3)):
                sp.dma_start(m.blk[:, n], w.rearrange("(k b) c d -> (b c) k d", k=NK)).then_inc(s.small_in, 16)
            sp.dma_start(m.wgate, a.w_gate_3.rearrange("(k p) g -> p k g", p=P)).then_inc(s.small_in, 16)
            sp.dma_start(m.bgate[0:8, :], a.b_gate_3.rearrange("(g o) -> g o", o=1)).then_inc(s.small_in, 16)
            for n in range(2):
                wt.load(sp, m.wbuf, chunk(a.w_in_3, n))
            for k in range(NK):
                sp.wait_ge(s.xc_ready, k + 1)
                sp.dma_start(a.xc_spill[k], xc[:, k, :]).then_inc(s.spilled, 16)
            for ap in following:
                wt.load(sp, m.wbuf, ap)

        @block.tensor
        def _(pe):
            for n in range(2):
                pe_split_chunk(pe, m, lambda k: m.R[3][:, 4 + k, :] if k < 4 else m.R[2][:, k, :], m.R[4], w_high[n],
                               split0 + 5 + n, False)
            for n in range(2):
                pe_feature_chunk(pe, m, m.xT)
            pe.wait_ge(wt.bank_free, NBANK + wt.outs)
            pe.wait_ge(s.small_in, 96)

            def blocks(k):
                pe.wait_ge(s.bd_ready, 3 * k + 3)
                pe.wait_ge(s.xc_ready, k + 1)
                for n, src in enumerate((xc, xc, xm)):
                    for half in range(2):
                        if n:
                            pe.wait_ge(s.qk_ready, 4 * k + 2 * (n - 1) + half + 1)
                        elif k:
                            pe.wait_ge(s.vt_ready, 2 * (k - 1) + half + 1)
                        pe.matmul(m.bank[:, 4 + half, :], bd[n], half_of(src, k, half),
                                  start=True, stop=True).then_inc(s.blk_done, 1)
                for half in range(2):
                    if k:
                        pe.wait_ge(s.v_ready, 2 * (k - 1) + half + 1)
                    for i in range(4):
                        tt = 4 * half + i
                        mm = pe.matmul(m.bank[:, 6 + half, i * P:(i + 1) * P], xm[:, k, tt * P:(tt + 1) * P], bd[2],
                                       start=True, stop=True)
                    mm.then_inc(s.v_done, 1)

            def gates(k):
                pe.wait_ge(s.qk_ready, 4 * k + 4)
                pe.wait_ge(s.vt_ready, 2 * k + 2)
                for n in range(3):
                    for half in range(2):
                        src = (half_of(q, k, half), half_of(xc, k, half), vT[(2 * k + half) % 4])[n]
                        mm = pe.matmul(m.bank[0:8, half, :], m.wgate[:, 8 * n + k, :], src,
                                       start=(k == 0 and n == 0), stop=(k == NK - 1 and n == 2), skip_group_check=True)
                mm.then_inc(s.gates_done, 1)
            for k in range(NK + 1):
                if k < NK:
                    blocks(k)
                if k:
                    gates(k - 1)

        @block.scalar
        def _(act):
            def silu(k):
                act.wait_ge(s.conv_ready, k + 1)
                act.activation(xc[:, k, :], xc[:, k, :], ACT.Silu).then_inc(s.xc_ready, 1)
            for n in range(16):
                act.wait_ge(wt.mm_done, base + 16 + n + 1)
                act.wait_ge(wt.bank_free, NBANK + base + 16)
                act.activation(half_of(xm, n // 2, n % 2), m.bank[:, (base + 16 + n) % NBANK, :], ACT.Copy)\
                    .then_inc(wt.bank_free, 1)
                if n % 2 and n >= 3:
                    silu(n // 2 - 1)
            silu(NK - 1)
            for k in range(NK):
                act.wait_ge(s.spilled, 16 * NK)
                for n in range(2):
                    for half in range(2):
                        act.wait_ge(s.blk_done, 6 * k + 2 * n + half + 1)
                        act.activation(half_of((q, xc)[n], k, half), m.bank[:, 4 + half, :], ACT.Copy).then_inc(s.qk_ready, 1)

        @block.gpsimd
        def _(pool):
            pool.wait_ge(s.small_in, 96)
            for k in range(NK):
                if k:
                    pool.wait_ge(s.v_done, 2 * k)
                for n in range(3):
                    ins = pool.tensor_tensor(bd[n].rearrange("p (b d) -> p b d", d=4),
                                             m.mask4.unsqueeze(2).broadcast_to([P, 32, 4]),
                                             m.blk[:, n, k:k + 1, :].broadcast_to([P, 32, 4]), ALU.mult)
                    ins.then_inc(s.bd_ready, 1)

        @block.vector
        def _(dve):
            for c, src in enumerate((m.R[3], m.R[2])):
                for half in range(2):
                    h = slice(half * HALF, (half + 1) * HALF)
                    split_operand(dve, m, src[:, 4:8, h], m.R[4][:, 4 * c:4 * c + 4, h])
                if c == 0:
                    split_weights(dve, m, n0, w_high[0])
            split_weights(dve, m, n0 + 1, w_high[1])
            m.splits += 6
            dve.wait_ge(m.x_back, 2 * 16 * NT)
            for n in range(2):
                for i in range(NT):
                    add_product(dve, m, i, n, base + NT * n).then_inc(wt.bank_free, 1)
            for k in range(NK):
                dve.wait_ge(wt.bank_free, NBANK + base + 16 + 2 * k + 2)
                y = xc[:, k, :]
                ins = dve.tensor_scalar(y, xm[:, k, :], m.c("conv_w", (CW - 1) * 8 + k), m.c("conv_b", k), ALU.mult, ALU.add)
                for lag in range(1, CW):
                    m.dve_link(dve, ins)
                    ins = dve.scalar_tensor_tensor(y[:, lag:S], xm[:, k, 0:S - lag], m.c("conv_w", (CW - 1 - lag) * 8 + k),
                                                   y[:, lag:S], op0=ALU.mult, op1=ALU.add)
                ins.then_inc(s.conv_ready, 1)
            for k in range(NK):
                for half in range(2):
                    if k >= 2:
                        dve.wait_ge(s.gates_done, k - 1)
                    dve.wait_ge(s.blk_done, 6 * k + 4 + half + 1)
                    dve.tensor_copy(vT[(2 * k + half) % 4], m.bank[:, 4 + half, :]).then_inc(s.vt_ready, 1)
                dve.wait_ge(s.v_done, 2 * k + 2)
                for half in range(2):
                    dve.tensor_copy(half_of(xm, k, half), m.bank[:, 6 + half, :]).then_inc(s.v_ready, 1)


def mlstm(nc, m, a, following):
    wt = m.wt
    q, k, v = m.R[2], m.R[3], m.R[4]
    rows, rows2 = m.gb[:, 0, :], m.gb[:, 1, :]
    slot = m.wbuf[:, (wt.used + 1) % 2].rearrange("p k n -> p (k n)")
    Dm, capped = [slot[:, 0:S], slot[:, S:2 * S]], [slot[:, 2 * S:2 * S + P], slot[:, 2 * S + P:2 * S + 2 * P]]
    Gb = slot[:, 2 * S + 2 * P:3 * S + 2 * P]
    upto = m.cst[:, 2, :]
    s = Names()
    s.upto_in, s.gates, s.split, s.abs = (
        m.sem("mx_upto_in"), m.sem("mx_gates"), m.sem("mx_split"), m.sem("mx_abs"))
    s.turned_a, s.turned_m, s.m_ready, s.a_rows = (
        m.sem("mx_turned_a"), m.sem("mx_turned_m"), m.sem("mx_m_ready"), m.sem("mx_a_rows"))
    s.a_cols, s.em_cols, s.gb_done, s.gb_copied = (
        m.sem("mx_a_cols"), m.sem("mx_em_cols"), m.sem("mx_gb_done"), m.sem("mx_gb_copied"))
    s.scores, s.capped, s.decay, s.weights = (
        m.sem("mx_scores"), m.sem("mx_capped"), m.sem("mx_decay"), m.sem("mx_weights"))
    s.av, s.h_ready = (
        m.sem("mx_av"), m.sem("mx_h_ready"))
    units = [(h, t) for h in range(M_HEADS) for t in range(NT - 1, -1, -1)]
    N = len(units)
    ac, em, den = m.a_cols, m.em_cols, m.den
    pair = lambda x, h, t: x[:, 2 * h:2 * h + 2, t * P:(t + 1) * P]

    with nc.Block() as block:
        @block.sync
        def _(sp):
            sp.dma_start(upto, a.upto).then_inc(s.upto_in, 16)
            for ap in following:
                wt.load(sp, m.wbuf, ap)

        @block.tensor
        def _(pe):
            pe.wait_ge(s.gates, 2)
            for n in range(2):
                for half in range(2):
                    mm = pe.matmul(m.bank[0:4, 2 + 2 * n + half, :], m.ident[0:8, 4 * n:4 * n + 4],
                                   rows[0:8, half * HALF:(half + 1) * HALF], start=True, stop=True)
            mm.then_inc(s.split, 1)
            cols = m.bank[:, 6:8, :].rearrange("p b n -> p (b n)")
            for src, ready, out, at in ((rows2, s.a_rows, s.turned_a, 0), (rows, s.m_ready, s.turned_m, HALF)):
                pe.wait_ge(ready, 1)
                for t in range(NT):
                    mm = pe.transpose(cols[:, at + 4 * t:at + 4 * t + 4], src[0:4, t * P:(t + 1) * P], m.ident[0:4, 0:4])
                mm.then_inc(out, 1)
            pe.wait_ge(s.em_cols, 1)
            pe.wait_ge(s.a_cols, 1)

            def scores(n):
                h, t = units[n]
                if t == NT - 1:
                    if h:
                        pe.wait_ge(s.gb_copied, h)
                    for half in range(2):
                        mm = pe.matmul(m.bank[:, 6 + half, :], m.ident[0:4, h:h + 1].broadcast_to([4, P]),
                                       rows2[0:4, half * HALF:(half + 1) * HALF], start=True, stop=True)
                    mm.then_inc(s.gb_done, 1)
                if n >= 2:
                    pe.wait_ge(s.weights, n - 1)
                for j in range(t + 1):
                    for c in range(2):
                        mm = pe.matmul(m.bank[:, 2 * (n % 2) + j // 4, (j % 4) * P:(j % 4 + 1) * P],
                                       k[:, 2 * h + c, j * P:(j + 1) * P], q[:, 2 * h + c, t * P:(t + 1) * P],
                                       start=(c == 0), stop=(c == 1))
                mm.then_inc(s.scores, 1)

            def values(n):
                h, t = units[n]
                pe.wait_ge(s.weights, n + 1)
                if n >= 2:
                    pe.wait_ge(s.h_ready, n - 1)
                bank = m.bank[:, 4 + n % 2, :]
                for j in range(t + 1):
                    w = Dm[n % 2][:, j * P:(j + 1) * P]
                    pe.matmul(bank[:, 0:2 * P].rearrange("p (c n) -> p c n", n=P), w, pair(v, h, j),
                              start=(j == 0), stop=False, skip_group_check=True)
                    mm = pe.matmul(bank[:, 2 * P:2 * P + 1], w, m.ones[:, 0:1], start=False, stop=(j == t),
                                   skip_group_check=True)
                mm.then_inc(s.av, 1)
            for n in range(N + 1):
                if n < N:
                    scores(n)
                if n:
                    values(n - 1)

        @block.scalar
        def _(act):
            act.preload_act_table_set(EXP_LN)
            act.wait_ge(s.split, 1)
            f = m.bank[0:4, 4:6, :].rearrange("p b n -> p (b n)")
            m.act_link(act, act.activation(rows2[0:4, :], f, ACT.Abs))
            m.act_link(act, act.activation(rows2[0:4, :], rows2[0:4, :], ACT.Exp, scale=-1.0))
            act.activation(rows2[0:4, :], rows2[0:4, :], ACT.Ln, bias=m.eps[0:4, 2:3]).then_inc(s.abs, 1)
            act.wait_ge(s.turned_a, 1)
            act.activation(ac, m.bank[:, 6, 0:32], ACT.Copy).then_inc(s.a_cols, 1)
            act.wait_ge(s.turned_m, 1)
            act.activation(em, m.bank[:, 7, 0:32], ACT.Exp, scale=-1.0).then_inc(s.em_cols, 1)
            act.wait_ge(s.em_cols, 1)
            act.wait_ge(s.a_cols, 1)
            for n in range(N):
                h, t = units[n]
                if t == NT - 1:
                    if h:
                        act.wait_ge(s.capped, NT * h)
                        act.wait_ge(s.decay, NT * h)
                    act.wait_ge(s.gb_done, h + 1)
                    act.activation(Gb, m.bank[:, 6:8, :].rearrange("p b n -> p (b n)"), ACT.Copy).then_inc(s.gb_copied, 1)
                act.wait_ge(s.gb_copied, h + 1)
                if n >= 2:
                    act.wait_ge(s.av, n - 1)
                for j in range(t):
                    act.activation(Dm[n % 2][:, j * P:(j + 1) * P], Gb[:, t * P:(t + 1) * P],
                                   ACT.Exp, scale=-1.0, bias=ac[:, 4 * j + h:4 * j + h + 1]).then_inc(m.act_link.sem, 1)
                    m.act_link.n += 1
                act.wait_ge(s.capped, n + 1)
                m.act_link(act, act.activation(Dm[n % 2][:, t * P:(t + 1) * P], capped[n % 2], ACT.Exp, scale=-1.0,
                                               bias=ac[:, 4 * t + h:4 * t + h + 1]))
                act.sem_inc(s.decay, 1)

        @block.vector
        def _(dve):
            for half in range(2):
                dve.wait_ge(m.ml_gates_done, NK)
                dve.tensor_scalar(rows[0:8, half * HALF:(half + 1) * HALF], m.bank[0:8, half, :], m.bgate[0:8, :], None,
                                  ALU.add).then_inc(s.gates, 1)
            dve.wait_ge(s.abs, 1)
            i_, f = (m.bank[0:4, b:b + 2, :].rearrange("p b n -> p (b n)") for b in (2, 4))
            m.dve_link(dve, dve.scalar_tensor_tensor(rows2[0:4, :], f, 0.0, rows2[0:4, :], op0=ALU.min, op1=ALU.subtract))
            m.dve_link(dve, dve.tensor_tensor_scan(rows[0:4, :], m.ones[0:4, 0:1].broadcast_to([4, S]), rows2[0:4, :], 0.0,
                                                   ALU.mult, ALU.add))
            dve.tensor_tensor(rows2[0:4, :], i_, rows[0:4, :], ALU.subtract).then_inc(s.a_rows, 1)
            dve.wait_ge(s.turned_a, 1)
            m.dve_link(dve, dve.tensor_tensor_scan(rows2[0:4, :], rows2[0:4, :], rows2[0:4, :], 0.0, ALU.max, ALU.max))
            dve.tensor_tensor(rows[0:4, :], rows[0:4, :], rows2[0:4, :], ALU.add).then_inc(s.m_ready, 1)
            dve.wait_ge(s.upto_in, 16)
            dve.wait_ge(s.a_cols, 1)
            dve.wait_ge(s.em_cols, 1)

            def cap(n):
                h, t = units[n]
                dve.wait_ge(s.gb_copied, h + 1)
                if n >= 2:
                    dve.wait_ge(s.decay, n - 1)
                dve.tensor_scalar(capped[n % 2], Gb[:, t * P:(t + 1) * P],
                                  ac[:, 4 * t + h:4 * t + h + 1], None, ALU.max).then_inc(s.capped, 1)

            def weights(n):
                h, t = units[n]
                w = (t + 1) * P
                d = Dm[n % 2]
                dve.wait_ge(s.decay, n + 1)
                m.dve_link(dve, dve.tensor_tensor(d[:, t * P:w], d[:, t * P:w], upto, ALU.mult))
                dve.wait_ge(s.scores, n + 1)
                src = m.bank[:, 2 * (n % 2):2 * (n % 2) + 2, :].rearrange("p b n -> p (b n)")[:, 0:w]
                dve.scalar_tensor_tensor(d[:, 0:w], src, 1.0 / 16, d[:, 0:w], op0=ALU.mult, op1=ALU.mult).then_inc(s.weights, 1)

            def out(n):
                h, t = units[n]
                dve.wait_ge(s.av, n + 1)
                bank = m.bank[:, 4 + n % 2, :]
                r = den[:, n % 2:n % 2 + 1]
                m.dve_link(dve, dve.tensor_scalar(r, bank[:, 2 * P:2 * P + 1], -1.0, em[:, 4 * t + h:4 * t + h + 1],
                                                  ALU.mult, ALU.max))
                m.dve_link(dve, dve.tensor_tensor(r, r, bank[:, 2 * P:2 * P + 1], ALU.max))
                m.dve_link(dve, dve.reciprocal(r, r))
                dve.tensor_scalar(pair(v, h, t), bank[:, 0:2 * P].rearrange("p (c n) -> p c n", n=P), r, None,
                                  ALU.mult).then_inc(s.h_ready, 1)
            cap(0)
            for n in range(N + 1):
                if n + 1 < N and units[n + 1][0] == units[n][0]:
                    cap(n + 1)
                if n < N:
                    weights(n)
                if n + 1 < N and units[n + 1][0] != units[n][0]:
                    cap(n + 1)
                if n:
                    out(n - 1)


def mlstm_out(nc, m, a):
    wt = m.wt
    wt.plan([8] * 6)
    base = wt.outs
    y, z, h = m.R[2], m.R[3], m.R[4]
    gate = [m.gb[:, 0, 0:HALF], m.gb[:, 0, HALF:S]]
    s = Names()
    s.e_ready, s.gated, s.var_ready, s.root_ready = (
        m.sem("mo_e_ready"), m.sem("mo_gated"), m.sem("mo_var_ready"), m.sem("mo_root_ready"))
    s.rows_ready, s.turned, s.headed, s.xc_in = (
        m.sem("mo_rows_ready"), m.sem("mo_turned"), m.sem("mo_headed"), m.sem("mo_xc_in"))
    s.skipped, s.y_ready, s.x_ready, s.x_root = (
        m.sem("mo_skipped"), m.sem("mo_y_ready"), m.sem("mo_x_ready"), m.sem("mo_x_root"))
    s.final, s.g_final_in = (
        m.sem("mo_final"), m.sem("mo_g_final_in"))
    stat = m.ho_stat
    stored = [m.sem(f"stored_{b}") for b in range(2)]
    out_rows = [m.R[4][:, 0, :], m.R[4][:, 1, :]]
    junk = [m.R[4][:, 2, :], m.R[4][:, 3, :]]
    M = NBANK + base
    w_high, split0 = [quarter(m.R[3], c) for c in range(2)], m.splits
    with nc.Block() as block:
        @block.sync
        def _(sp):
            for n in range(1, 6):
                wt.load(sp, m.wbuf, (chunk(a.w_in_3, 4 + n) if n < 2 else chunk(a.w_in_3, n) if n < 4
                                     else chunk(a.w_out_3, n - 4)))
                if n == 3:
                    for k in range(NK):
                        sp.wait_ge(s.turned, 2 * k + 2)
                        sp.dma_start(h[:, k, :], a.xc_spill[k]).then_inc(s.xc_in, 16)
            sp.wait_ge(s.turned, 2 * NK)
            sp.dma_start(m.gb[:, 1, :], a.g_final_3.partition_broadcast(P)).then_inc(s.g_final_in, 16)
            for i in range(NT):
                sp.wait_ge(s.final, i + 1)
                sp.dma_start(a.out[0, i * P:(i + 1) * P, :], out_rows[i % 2]).then_inc(stored[i % 2], 16)
            for b in range(2):
                sp.wait_ge(stored[b], 16 * NT // 2)

        @block.tensor
        def _(pe):
            for n in range(2):
                pe_token_chunk(pe, m, m.xT)

            def turn(n):
                pe.wait_ge(s.rows_ready, 2 * NT)
                if n >= 2:
                    pe.wait_ge(s.headed, n - 1)
                for i in range(4):
                    t = 4 * (n % 2) + i
                    mm = pe.transpose(m.bank[:, 6 + n % 2, i * P:(i + 1) * P], h[:, n // 2, t * P:(t + 1) * P], m.ident)
                mm.then_inc(s.turned, 1)
            pe_feature_chunk(pe, m, m.xT, wait_before=lambda g: turn(2 * (g - 1)) or turn(2 * (g - 1) + 1) if g else None)
            pe_feature_chunk(pe, m, m.xT, wait_before=lambda g: turn(14) or turn(15) if g == 0 else None)
            pe.wait_ge(s.y_ready, NK)
            for n in range(2):
                pe_split_chunk(pe, m, y, m.R[1], w_high[n], split0 + 3 + n, False, n == 0)

        @block.scalar
        def _(act):
            act.preload_act_table_set(EXP_LN)

            def root(u):
                act.wait_ge(s.var_ready, u + 1)
                v = stat[:, u % 2, :, 1:2]
                m.act_link(act, act.activation(v, v, ACT.Ln, bias=m.eps_col(RMS_EPS)))
                act.activation(v, v, ACT.Exp, scale=-0.5).then_inc(s.root_ready, 1)
            for u in range(2 * NT):
                act.wait_ge(wt.mm_done, base + u + 1)
                if u >= 2:
                    act.wait_ge(s.gated, u - 1)
                act.activation(gate[u % 2], m.bank[:, (base + u) % NBANK, :], ACT.Exp, scale=-1.0).then_inc(wt.bank_free, 1)
                if u:
                    root(u - 1)
            root(2 * NT - 1)
            for n in range(16):
                act.wait_ge(wt.mm_done, base + 16 + n + 1)
                act.activation(z[:, n // 2, (n % 2) * HALF:(n % 2 + 1) * HALF], m.bank[:, (base + 16 + n) % NBANK, :],
                               ACT.Silu).then_inc(wt.bank_free, 1)
            for i in range(NT):
                xr = m.xroot[:, i % 2]
                act.wait_ge(s.x_ready, i + 1)
                m.act_link(act, act.activation(junk[i % 2], m.X[:, i, :], ACT.Square, accum_out=xr[:, 0:1]))
                act.activation(xr[:, 1:2], xr[:, 0:1], ACT.Sqrt, scale=1.0 / D, bias=m.eps_col(RMS_EPS)).then_inc(s.x_root, 1)

        @block.gpsimd
        def _(pool):
            for k in range(NK):
                pool.wait_ge(s.skipped, k + 1)
                pool.wait_ge(wt.bank_free, M + 16 + 2 * k + 2)
                pool.tensor_tensor(y[:, k, :], y[:, k, :], z[:, k, :], ALU.mult).then_inc(s.y_ready, 1)

        @block.vector
        def _(dve):
            def gated(u):
                n, i = u // NT, u % NT
                e = gate[u % 2]
                hh = h[:, 4 * n:4 * n + 4, i * P:(i + 1) * P]
                dve.wait_ge(wt.bank_free, M + u + 1)
                m.dve_link(dve, dve.tensor_scalar(e, e, 1.0, None, ALU.add))
                m.dve_link(dve, dve.reciprocal(e, e))
                dve.tensor_tensor(hh, hh, e.rearrange("p (c n) -> p c n", n=P), ALU.mult).then_inc(s.gated, 1)
                dve.wait_ge(s.gated, u + 1)
                for c in range(2):
                    m.dve_link(dve, dve.bn_stats(m.stats[:, c, 0, :], hh[:, 2 * c:2 * c + 2, :]))
                for c in range(2):
                    m.dve_link(dve, dve.bn_aggr(stat[:, u % 2, c, 0:2], m.stats[:, c, 0, :]))
                dve.sem_inc(s.var_ready, 1)

            def normed(u):
                n, i = u // NT, u % NT
                dve.wait_ge(s.root_ready, u + 1)
                for c in range(2):
                    x = h[:, 4 * n + 2 * c:4 * n + 2 * c + 2, i * P:(i + 1) * P]
                    m.dve_link(dve, dve.tensor_scalar(x, x, stat[:, u % 2, c, 0:1], stat[:, u % 2, c, 1:2],
                                                      ALU.subtract, ALU.mult))
                dve.sem_inc(s.rows_ready, 1)
            for u in range(2 * NT + 1):
                if u < 2 * NT:
                    gated(u)
                if u:
                    normed(u - 1)
            for n in range(16 + 2):
                if n < 16:
                    dve.wait_ge(s.turned, n + 1)
                    dve.tensor_scalar(y[:, n // 2, (n % 2) * HALF:(n % 2 + 1) * HALF], m.bank[:, 6 + n % 2, :],
                                      m.c("g_head", n // 2), None, ALU.mult).then_inc(s.headed, 1)
            for k in range(NK):
                dve.wait_ge(s.xc_in, 16 * NK)
                dve.wait_ge(s.headed, 2 * k + 2)
                dve.scalar_tensor_tensor(y[:, k, :], h[:, k, :], m.c("skip", k), y[:, k, :], op0=ALU.mult,
                                         op1=ALU.add).then_inc(s.skipped, 1)
            dve.wait_ge(s.y_ready, NK)
            split_first(dve, m, y, m.R[1], wt.used - 2, w_high[0])
            split_weights(dve, m, wt.used - 1, w_high[1])
            m.splits += 4
            for i in range(NT):
                add_product(dve, m, i, 0, base + 32).then_inc(wt.bank_free, 1)
            dve.wait_ge(s.g_final_in, 16)

            def final(i):
                xr = m.xroot[:, i % 2]
                dve.wait_ge(s.x_root, i + 1)
                if i >= 2:
                    dve.wait_ge(stored[i % 2], 16 * (i // 2))
                m.dve_link(dve, dve.reciprocal(xr[:, 2:3], xr[:, 1:2]))
                dve.scalar_tensor_tensor(out_rows[i % 2], m.X[:, i, :], xr[:, 2:3], m.gb[:, 1, :], op0=ALU.mult,
                                         op1=ALU.mult).then_inc(s.final, 1)
            for i in range(NT):
                add_product(dve, m, i, 1, base + 40).then_inc(wt.bank_free, 1)
                dve.wait_ge(wt.bank_free, M + 40 + i + 1)
                dve.sem_inc(s.x_ready, 1)
                if i:
                    final(i - 1)
            final(NT - 1)


def tables():
    i = np.arange(P)
    c = np.zeros((P, 7, P), np.float32)
    c[:, 0] = np.eye(P)
    c[:, 1] = 1.0
    c[:, 2] = -(i[:, None] >= i[None, :]).astype(np.float32)
    c[:, 3] = i[:, None] < i[None, :]
    c[:, 4] = np.where(i[:, None] < i[None, :], 3e38, -1e4)
    c[:, 5] = (i[:, None] // HEAD_DIM == i[None, :] // HEAD_DIM) / HEAD_DIM
    c[:, 6] = -1.0
    fix = np.ones((P, 4, 16), np.float32)
    for g, w in enumerate(POOL_WINDOWS):
        fix[:, g, :w] = w / (np.arange(w) + 1.0)
    levels = np.zeros((P, 8, P), np.float32)
    levels[:, 0] = np.eye(P)
    for n, w in enumerate(LEVELS):
        block, late = i // (2 * w), i // w % 2
        levels[:, n + 1] = (block[:, None] == block[None, :]) & (late[:, None] == 0) & (late[None, :] == 1)
    half = ROPE_DIM // 2
    inv = 500000.0 ** (-np.arange(0, ROPE_DIM, 2, dtype=np.float32) / np.float32(ROPE_DIM))
    angle = np.arange(S, dtype=np.float32)[None, :] * inv.astype(np.float32)[:, None]
    rope, swap = np.zeros((2, P, S), np.float32), np.zeros((P, P), np.float32)
    rope[0] = 1.0
    for head in (0, A_DIM):
        for part in (0, half):
            rope[0, head + part:head + part + half] = np.cos(angle)
            rope[1, head + part:head + part + half] = np.sin(angle)
        for n in range(half):
            swap[head + half + n, head + n] = -1.0
            swap[head + n, head + half + n] = 1.0
    dist = (NT - 1) * P + i[:, None] - np.arange(S)[None, :]
    count = np.zeros((P, S))
    for window, dil in ((128, 1), (512, 4), (2048, 16)):
        count += (dist >= 0) & (dist % dil == 0) & (dist <= window)
    logc = np.where(count > 0, np.log(np.maximum(count, 1)), -1e30).astype(np.float32)
    mask4 = (i[:, None] // 4 == np.arange(32)[None, :]).astype(np.float32)
    upto = (i[:, None] <= i[None, :]).astype(np.float32)
    return {"consts": c, "pool_fix": fix, "level_masks": levels, "rope": rope, "rope_swap": swap, "log_count": logc,
            "mask4": mask4, "upto": upto}


def build(nc, a):
    with nc.allow_non_contiguous_dma(reason="weight chunks"):
        def sem(name):
            return nc.alloc_semaphore(name)

        def sb(name, *shape):
            return nc.alloc_sbuf_tensor(name, [P, *shape], F32)
        m = Names()
        m.sem, m.pe = sem, nc.tensor
        m.wt = Weights(nc, sem)
        split_view = {}

        def sb_split(name, *shape):
            t = sb(name, *shape)
            at = nc.sbuf_base - 4 * int(np.prod(shape))
            split_view[name] = nc.alloc_sbuf_tensor_at(name + "_parts", [P, *shape], F32R, offset=at)
            return t
        m.parts = lambda ap: bass.AP(split_view[ap.tensor.name], ap.offset, ap.ap)
        m.R = [sb_split(f"region{r}", NK, S) for r in range(5)]
        m.X, m.xT = m.R[0], m.R[1]
        m.wbuf = sb_split("weight_chunks", 2, NK, COLS)
        m.gb = sb("gain_offset", 2, D)
        m.cst = sb("constants", 7, P)
        m.ident, m.ones, m.negtri, m.before, m.cap, m.headmean, m.negones = (m.cst[:, t, :] for t in range(7))
        m.poolfix = sb("pool_fix", 4, 16)
        m.eps = sb("small_numbers", 4)
        m.stats = sb("stats", 2, 2, 6)
        m.mv = sb("mean_var_root", 2, 4)
        m.bank = nc.alloc_psum_tensor("banks", [P, 8, HALF], F32)
        m.gb_in, m.gb_count = sem("gain_offset_in"), 0
        m.dve_link, m.act_link, m.pool_link = Link(sem("vector_link")), Link(sem("scalar_link")), Link(sem("gpsimd_link"))
        m.eps_col = lambda e: m.eps[:, (LN_EPS, RMS_EPS, 1.0).index(e):(LN_EPS, RMS_EPS, 1.0).index(e) + 1]
        m.q1, m.k1 = m.R[2][:, 0:4, :], m.R[2][:, 4:8, :]
        m.v1 = m.R[3][:, 0:4, :].rearrange("p a (b n) -> p (a b) n", n=COLS)
        m.u1, m.mixT = m.R[3][:, 4:8, :], m.R[4]
        m.order1 = (0, 1, 2, 3)
        m.c_act, m.mod, m.xroot, m.lbt = sb("silu_c", 8)[:], sb("modulation", 48)[:], sb("x_root", 2, 3)[:], sb("lower_bound", 12)[:]
        m.i2, m.Y = m.R[4][:, 0:4, :].rearrange("p a (b n) -> p (a b) n", n=COLS), m.R[3]

        where, at = {}, 0
        m.vectors, m.n_rows, m.col_at = [], [], []
        for group in a.columns:
            rows, r = [], 0
            for name, ap, n in group:
                rows.append((ap, r, n))
                where[name] = at + r
                r += n
            m.vectors.append(rows)
            m.n_rows.append(r)
            m.col_at.append(at)
            at += r
        m.col = sb("columns", at)
        m.c = lambda name, k: m.col[:, where[name] + k:where[name] + k + 1]
        m.va = m.R[3][:, 0:4, :].rearrange("p a (b n) -> p (a b) n", n=COLS)
        m.da_stat, m.xa_stat, m.ho_stat = sb("dilated_stats", 3, 4)[:], sb("cross_stats", 2, 12)[:], sb("head_stats", 2, 2, 2)[:]
        m.mask4, m.blk, m.wgate = sb("mask4", 32)[:], sb("blocks", 3, NK, 4)[:], sb("w_gate", 24, 8)[:]
        m.bgate, m.a_cols, m.em_cols, m.den = sb("b_gate", 1)[:], sb("a_columns", 32)[:], sb("exp_m_columns", 32)[:], sb("den", 2)[:]
        a.xc_spill = nc.dram_tensor("xc_spill", (NK, P, S), F32, kind="Internal").ap()
        m.split_done, m.splits = sem("split_done"), 0
        m.spilled, m.x_back = sem("x_spilled"), sem("x_back")
        a.x_spill = nc.dram_tensor("x_spill", (NT, P, D), F32, kind="Internal").ap()
        m.cols = lambda name, k, n: m.col[:, where[name] + k:where[name] + k + n]
        stages(nc, m, a)


def stages(nc, m, a):
    up1 = [chunk(a.w_up, 0), down_chunk(a.w_down, 0)]
    own = nc.snapshot_sems()
    embed_norm(nc, m, a, [chunk(a.w_in, c) for c in range(2)])
    ada = [chunk(a.w_ada_2, c) for c in range(12)]
    project_1(nc, m, a, ada[:2])
    attention_1(nc, m, a, ada[2:], [chunk(a.w_out, c) for c in range(2)])
    mix_out_1(nc, m, a, up1)
    feed_forward(nc, m, a.w_up, a.w_down, [chunk(a.w_ple_gate, c) for c in range(2)], m.X,
                 NormTail(m, Norm(m, "ln2", LN_EPS), a.ln2_g, a.ln2_b), "ffn1", m.R[3])
    per_layer_embedding(nc, m, a, [chunk(a.w_in_2, c) for c in range(2)])
    project_2(nc, m, a, [chunk(a.w_out_2, c) for c in range(2)])
    group_norm_and_hgrn(nc, m, a)
    mix_out_2(nc, m, a, [chunk(a.w_up_2, 0), down_chunk(a.w_down_2, 0)])
    feed_forward(nc, m, a.w_up_2, a.w_down_2, [chunk(a.w_in_3, c) for c in (6, 7)], m.Y,
                 Tail(m, "post_ffn", "gated rms", m.cols("g_norm", 0, 8), None, gate=m.gb[:, 1, :], at=0), "ffn2", m.X,
                 m.spilled, a.x_spill, zero=True)
    project_attention(nc, m, a, [chunk(a.w_mem_kv_3, c) for c in range(2)])
    nc.clear_and_free_semaphores(nc.allocated_since(own))
    nc.all_engine_barrier()
    dilated_attention(nc, m, a)
    cross_attention(nc, m, a, [chunk(a.w_out_3, c, rows=D) for c in range(2)])
    attention_out(nc, m, a, [chunk(a.w_in_3, 4)])
    mlstm(nc, m, a, [])
    mlstm_out(nc, m, a)


def inputs(t):
    a = Names()
    a.w_in, a.attn_out_g, a.pool_scale = t["w_in"][0], t["attn_out_g"][0], t["pool_scale"][0]
    a.w_out, a.ln1_g, a.ln1_b = t["w_out"][0], t["ln1_g"][0], t["ln1_b"][0]
    a.w_up, a.w_down, a.ln2_g = t["w_up"][0], t["w_down"][0], t["ln2_g"][0]
    a.ln2_b, a.w_ple_gate, a.ln3_g = t["ln2_b"][0], t["w_ple_gate"][0], t["ln3_g"][0]
    a.ln3_b, a.c_2, a.w_ada_2 = t["ln3_b"][0], t["c_2"][0], t["w_ada_2"][0]
    a.b_ada_2, a.g_pre_mix_2, a.w_in_2 = t["b_ada_2"][0], t["g_pre_mix_2"][0], t["w_in_2"][0]
    a.b_in_2, a.w_dw_2, a.b_dw_2 = t["b_in_2"][0], t["w_dw_2"][0], t["b_dw_2"][0]
    a.gn_gain_2, a.gn_bias_2, a.g_hgrn_out_2 = t["gn_gain_2"][0], t["gn_bias_2"][0], t["g_hgrn_out_2"][0]
    a.w_out_2, a.g_post_mix_2, a.g_pre_ffn_2 = t["w_out_2"][0], t["g_post_mix_2"][0], t["g_pre_ffn_2"][0]
    a.w_up_2, a.w_down_2, a.g_post_ffn_2 = t["w_up_2"][0], t["w_down_2"][0], t["g_post_ffn_2"][0]
    a.mem_3, a.g_norm_3, a.w_in_3 = t["mem_3"][0], t["g_norm_3"][0], t["w_in_3"][0]
    a.conv_w_3, a.conv_b_3, a.w_q_blk_3 = t["conv_w_3"][0], t["conv_b_3"][0], t["w_q_blk_3"][0]
    a.w_k_blk_3, a.w_v_blk_3, a.w_gate_3 = t["w_k_blk_3"][0], t["w_v_blk_3"][0], t["w_gate_3"][0]
    a.b_gate_3, a.g_head_3, a.skip_3 = t["b_gate_3"][0], t["g_head_3"][0], t["skip_3"][0]
    a.g_mem_3, a.w_mem_kv_3, a.w_out_3 = t["g_mem_3"][0], t["w_mem_kv_3"][0], t["w_out_3"][0]
    a.x, a.p, a.emb_ln_g = t["x"], t["p"], t["emb_ln_g"]
    a.emb_ln_b, a.w_pool, a.w_ple = t["emb_ln_b"], t["w_pool"], t["w_ple"]
    a.lb_logits_2, a.g_final_3, a.consts = t["lb_logits_2"], t["g_final_3"], t["consts"]
    a.pool_fix, a.level_masks, a.rope = t["pool_fix"], t["level_masks"], t["rope"]
    a.rope_swap, a.log_count, a.mask4 = t["rope_swap"], t["log_count"], t["mask4"]
    a.upto = t["upto"]

    def rows(v):
        return v.rearrange("(k p) -> k p", p=P)
    a.columns = [
        [("attn_out_g", rows(a.attn_out_g), 4), ("pool_scale", rows(a.pool_scale), 4),
         ("g_pre_mix", rows(a.g_pre_mix_2), 8), ("b_ada", rows(a.b_ada_2), 48), ("c", rows(a.c_2), 8),
         ("g_pre_ffn", rows(a.g_pre_ffn_2), 8), ("lb_logits", a.lb_logits_2.rearrange("l (k p) -> (l k) p", p=P), 8),
         ("g_hgrn_out", rows(a.g_hgrn_out_2), 4), ("gn_gain", rows(a.gn_gain_2), 4), ("gn_bias", rows(a.gn_bias_2), 4),
         ("b_dw", rows(a.b_dw_2), 4), ("b_in_2", rows(a.b_in_2), 24)],
        [("w_dw", a.w_dw_2.rearrange("w (k p) -> (w k) p", p=P), 124)],
        [("conv_w", a.conv_w_3.rearrange("w (k p) -> (w k) p", p=P), 32), ("conv_b", rows(a.conv_b_3), 8),
         ("g_head", rows(a.g_head_3), 8), ("skip", rows(a.skip_3), 8), ("g_norm", rows(a.g_norm_3), 8),
         ("g_mem", rows(a.g_mem_3), 8), ("g_post_mix", rows(a.g_post_mix_2), 8), ("g_post_ffn", rows(a.g_post_ffn_2), 8)],
    ]
    return a


def kernel(**arrays_in):
    import numpy as _np
    import concourse.bacc as _bacc
    from concourse import mybir as _mybir
    from concourse.bass_utils import run_bass_kernel_spmd as _run

    nc = _bacc.Bacc("TRN2", target_bir_lowering=False, num_devices=1)
    arrays, tensors = {}, {}
    for name, value in {**arrays_in, **tables()}.items():
        value = _np.ascontiguousarray(value)
        arrays["in_" + name] = value
        tensors[name] = nc.dram_tensor("in_" + name, value.shape, _mybir.dt.from_np(value.dtype), kind="ExternalInput").ap()
    a = inputs(tensors)
    a.out = nc.dram_tensor("out", (1, S, D), _mybir.dt.float32, kind="ExternalOutput").ap()
    build(nc, a)
    return _run(nc, [arrays], core_ids=[0]).results[0]["out"]
```
